# Optimizing a Trainium2 kernel written in Bass

```python
import math
import jax, jax.numpy as jnp
from jax import lax
import numpy as np

D_MODEL = 1024
BATCH = 1
SEQ = 1024
DEPTH = 1

SSM_WIDTH = D_MODEL // 2
SSM_GROUP = 16
SSM_GROUPS = SSM_WIDTH // SSM_GROUP
SSM_STATE = 64
SSM_CHUNK_MAX = 512
DT_MIN = 1e-3
DT_MAX = 1e-1
ATTN_HEADS = 8
HEAD_DIM = 64
ATTN_WIDTH = ATTN_HEADS * HEAD_DIM
IDX_HEADS = 8
IDX_DIM = 64
IDX_SCALE = (IDX_HEADS * IDX_DIM) ** -0.5
TOPK_MAX = 256
Q_BLOCK = 128
RMS_EPS = 1e-6

IN_WIDTHS = (
    SSM_WIDTH,
    SSM_WIDTH,
    ATTN_WIDTH,
    HEAD_DIM,
    HEAD_DIM,
    ATTN_WIDTH,
    IDX_HEADS * IDX_DIM,
    IDX_DIM,
    IDX_HEADS,
    D_MODEL,
    D_MODEL,
)
IN_COLS = sum(IN_WIDTHS)
IN_SPLITS = tuple(int(s) for s in np.cumsum(IN_WIDTHS)[:-1])


def rms_norm(x, g):
    x32 = x.astype(jnp.float32)
    y = x32 * lax.rsqrt(jnp.mean(x32 * x32, axis=-1, keepdims=True) + RMS_EPS)
    return (y * g.astype(jnp.float32)).astype(x.dtype)

def _complex_affine_combine(e1, e2):
    a1r, a1i, b1r, b1i = e1
    a2r, a2i, b2r, b2i = e2
    return (a1r * a2r - a1i * a2i,
            a1r * a2i + a1i * a2r,
            a2r * b1r - a2i * b1i + b2r,
            a2r * b1i + a2i * b1r + b2i)

def s5_mixer(u, a_re, a_im, b_re, b_im, c_re, c_im, d_skip, log_dt):
    bsz, seq_len, _ = u.shape
    f32 = jnp.float32
    ar, ai = a_re.astype(f32), a_im.astype(f32)
    dt = jnp.exp(log_dt.astype(f32))[:, None]
    mag = jnp.exp(ar * dt)
    abar_r, abar_i = mag * jnp.cos(ai * dt), mag * jnp.sin(ai * dt)
    den = ar * ar + ai * ai
    nr = abar_r - 1.0
    cr = (nr * ar + abar_i * ai) / den
    ci = (abar_i * ar - nr * ai) / den
    br, bi = b_re.astype(f32), b_im.astype(f32)
    bb_r = cr[..., None] * br - ci[..., None] * bi
    bb_i = cr[..., None] * bi + ci[..., None] * br
    cre, cim = c_re.astype(f32), c_im.astype(f32)

    chunk = math.gcd(seq_len, SSM_CHUNK_MAX)
    n_chunks = seq_len // chunk
    ug = u.astype(f32).reshape(bsz, n_chunks, chunk, SSM_GROUPS, SSM_GROUP)
    ug = ug.transpose(1, 0, 2, 3, 4)

    def chunk_step(h0, u_c):
        h0r, h0i = h0
        bu_r = jnp.einsum('btgp,gnp->btgn', u_c, bb_r)
        bu_i = jnp.einsum('btgp,gnp->btgn', u_c, bb_i)
        a_r = jnp.broadcast_to(abar_r, bu_r.shape)
        a_i = jnp.broadcast_to(abar_i, bu_i.shape)
        cum_r, cum_i, hl_r, hl_i = lax.associative_scan(
            _complex_affine_combine, (a_r, a_i, bu_r, bu_i), axis=1)
        h_r = hl_r + cum_r * h0r[:, None] - cum_i * h0i[:, None]
        h_i = hl_i + cum_r * h0i[:, None] + cum_i * h0r[:, None]
        y = (jnp.einsum('btgn,gpn->btgp', h_r, cre)
             - jnp.einsum('btgn,gpn->btgp', h_i, cim))
        return (h_r[:, -1], h_i[:, -1]), y

    h_init = (jnp.zeros((bsz, SSM_GROUPS, SSM_STATE), f32),
              jnp.zeros((bsz, SSM_GROUPS, SSM_STATE), f32))
    _, y = lax.scan(chunk_step, h_init, ug)
    y = y.transpose(1, 0, 2, 3, 4).reshape(bsz, seq_len, SSM_WIDTH)
    y = y + d_skip.astype(f32) * u.astype(f32)
    return y.astype(u.dtype)

def dsa_mixer(q, k, v, q_idx, k_idx, w_idx):
    bsz, seq_len = q.shape[0], q.shape[1]
    f32 = jnp.float32
    top_k = min(TOPK_MAX, seq_len // 4)
    n_blocks = seq_len // Q_BLOCK
    key_pos = jnp.arange(seq_len)
    k_idx32 = k_idx.astype(f32)
    attn_scale = HEAD_DIM ** -0.5

    def to_blocks(t):
        return t.reshape((bsz, n_blocks, Q_BLOCK) + t.shape[2:]).swapaxes(0, 1)

    def block(args):
        blk, qb, qib, wb = args
        q_pos = blk * Q_BLOCK + jnp.arange(Q_BLOCK)
        causal = key_pos[None, :] <= q_pos[:, None]
        s = jax.nn.relu(jnp.einsum('bqhd,bkd->bqhk', qib.astype(f32), k_idx32)) * IDX_SCALE
        score = jnp.einsum('bqh,bqhk->bqk', wb.astype(f32), s)
        score = jnp.where(causal[None], score, -jnp.inf)
        _, sel = lax.top_k(score, top_k)
        valid = sel <= q_pos[None, :, None]
        k_sel = jax.vmap(lambda kk, ii: kk[ii])(k, sel)
        v_sel = jax.vmap(lambda vv, ii: vv[ii])(v, sel)
        logits = jnp.einsum('bqhd,bqkd->bqhk', qb.astype(f32), k_sel.astype(f32)) * attn_scale
        logits = jnp.where(valid[:, :, None, :], logits, -jnp.inf)
        p = jax.nn.softmax(logits, axis=-1)
        o = jnp.einsum('bqhk,bqkd->bqhd', p, v_sel.astype(f32))
        return o.astype(qb.dtype)

    out = lax.map(block, (jnp.arange(n_blocks), to_blocks(q), to_blocks(q_idx), to_blocks(w_idx)))
    return out.swapaxes(0, 1).reshape(bsz, seq_len, ATTN_WIDTH)

def hybrid_layer(x, c, norm_g, w_mod, b_mod, w_in, a_re, a_im, b_re, b_im, c_re, c_im,
                 d_skip, log_dt, w_glu, b_glu, w_a_o, w_b_o, w_out):
    bsz, seq_len, _ = x.shape
    mod = jax.nn.silu(c) @ w_mod + b_mod
    shift, scale, gate = jnp.split(mod, 3, axis=-1)
    h = rms_norm(x, norm_g) * (1 + scale[:, None]) + shift[:, None]
    proj = h @ w_in
    xa, za, q, k, v, zb, qi, ki, wi, ga, gb = jnp.split(proj, IN_SPLITS, axis=-1)

    ya = jax.nn.gelu(s5_mixer(xa, a_re, a_im, b_re, b_im, c_re, c_im, d_skip, log_dt))
    g = ya @ w_glu + b_glu
    ya = g[..., :SSM_WIDTH] * jax.nn.sigmoid(g[..., SSM_WIDTH:])
    ya = (ya * jax.nn.silu(za)) @ w_a_o

    yb = dsa_mixer(q.reshape(bsz, seq_len, ATTN_HEADS, HEAD_DIM), k, v,
                   qi.reshape(bsz, seq_len, IDX_HEADS, IDX_DIM), ki, wi)
    yb = (yb * jax.nn.silu(zb)) @ w_b_o

    merged = jax.nn.sigmoid(ga) * ya + jax.nn.sigmoid(gb) * yb
    return x + gate[:, None] * (merged @ w_out)

def first_inputs(seed: int = 0) -> dict:
    key = jax.random.key(seed)
    ks = jax.random.split(key, 20)
    f32 = jnp.float32
    G, N, P = SSM_GROUPS, SSM_STATE, SSM_GROUP

    def nrm(k, shape, std):
        return jax.random.normal(k, shape, f32) * std

    n_idx = jnp.arange(N, dtype=f32)
    return {
        "x": nrm(ks[0], (BATCH, SEQ, D_MODEL), 1.0),
        "c": nrm(ks[1], (BATCH, D_MODEL), 1.0),
        "norm_g": 1.0 + nrm(ks[2], (DEPTH, D_MODEL), 0.02),
        "w_mod": nrm(ks[3], (DEPTH, D_MODEL, 3 * D_MODEL), 0.5 * D_MODEL ** -0.5),
        "b_mod": nrm(ks[4], (DEPTH, 3 * D_MODEL), 0.01),
        "w_in": nrm(ks[5], (DEPTH, D_MODEL, IN_COLS), D_MODEL ** -0.5),
        "a_re": -0.5 + nrm(ks[6], (DEPTH, G, N), 0.01),
        "a_im": math.pi * n_idx + nrm(ks[7], (DEPTH, G, N), 0.01),
        "b_re": nrm(ks[8], (DEPTH, G, N, P), (2 * P) ** -0.5),
        "b_im": nrm(ks[9], (DEPTH, G, N, P), (2 * P) ** -0.5),
        "c_re": nrm(ks[10], (DEPTH, G, P, N), N ** -0.5),
        "c_im": nrm(ks[11], (DEPTH, G, P, N), N ** -0.5),
        "d_skip": nrm(ks[12], (DEPTH, SSM_WIDTH), 1.0),
        "log_dt": jax.random.uniform(ks[13], (DEPTH, G), f32,
                                     minval=math.log(DT_MIN), maxval=math.log(DT_MAX)),
        "w_glu": nrm(ks[14], (DEPTH, SSM_WIDTH, 2 * SSM_WIDTH), SSM_WIDTH ** -0.5),
        "b_glu": nrm(ks[15], (DEPTH, 2 * SSM_WIDTH), 0.01),
        "w_a_o": nrm(ks[16], (DEPTH, SSM_WIDTH, D_MODEL), SSM_WIDTH ** -0.5),
        "w_b_o": nrm(ks[17], (DEPTH, ATTN_WIDTH, D_MODEL), ATTN_WIDTH ** -0.5),
        "w_out": nrm(ks[18], (DEPTH, D_MODEL, D_MODEL), D_MODEL ** -0.5),
        "final_g": 1.0 + nrm(ks[19], (D_MODEL,), 0.02),
    }

def first_block(x, c, norm_g, w_mod, b_mod, w_in, a_re, a_im, b_re, b_im, c_re, c_im,
              d_skip, log_dt, w_glu, b_glu, w_a_o, w_b_o, w_out, final_g):
    for l in range(DEPTH):
        x = hybrid_layer(x, c, norm_g[l], w_mod[l], b_mod[l], w_in[l], a_re[l], a_im[l],
                         b_re[l], b_im[l], c_re[l], c_im[l], d_skip[l], log_dt[l],
                         w_glu[l], b_glu[l], w_a_o[l], w_b_o[l], w_out[l])
    return rms_norm(x, final_g)


D_MIX = 2 * D_MODEL
D_ATT = D_MIX // 2
ATT_HEAD_DIM = 64
ATT_HEADS = D_ATT // ATT_HEAD_DIM
ATT_STEPS = 128
DILATIONS = (1, 4, 16)
D_SSM = D_MIX - D_ATT
SSM_HEAD_DIM = 64
SSM_HEADS = D_SSM // SSM_HEAD_DIM
SSM_GROUPS_2 = 2
SSM_STATE_2 = 128
CONV_WIDTH = 4
CHUNK = 128
D_CONV = D_SSM + 2 * SSM_GROUPS_2 * SSM_STATE_2
D_IN_PROJ = 4 * D_ATT + D_SSM + D_CONV + SSM_HEADS
SPLITS = (D_ATT, 2 * D_ATT, 3 * D_ATT, 4 * D_ATT, 4 * D_ATT + D_SSM, 4 * D_ATT + D_SSM + D_CONV)
NORM_EPS = 1e-5


def rms_norm_2(u, g):
    uf = u.astype(jnp.float32)
    uf = uf * lax.rsqrt(jnp.mean(uf * uf, axis=-1, keepdims=True) + NORM_EPS)
    return (uf * g.astype(jnp.float32)).astype(u.dtype)

def layer_norm(u, g, b):
    uf = u.astype(jnp.float32)
    mu = jnp.mean(uf, axis=-1, keepdims=True)
    var = jnp.mean(jnp.square(uf - mu), axis=-1, keepdims=True)
    out = (uf - mu) * lax.rsqrt(var + NORM_EPS) * g.astype(jnp.float32) + b.astype(jnp.float32)
    return out.astype(u.dtype)

def alibi_slopes(n_heads):
    return jnp.asarray(2.0 ** (-8.0 * np.arange(1, n_heads + 1) / n_heads), dtype=jnp.float32)

def dilated_window_attention(q, k, v, slopes, dilation):
    B, S, H, E = q.shape
    unit = dilation * ATT_STEPS
    s_pad = -(-S // unit) * unit
    nb = s_pad // unit
    pad = ((0, 0), (0, s_pad - S), (0, 0), (0, 0))

    def to_blocks(t):
        return jnp.pad(t, pad).reshape(B, nb, ATT_STEPS, dilation, H, E)

    def with_prev(t):
        prev = jnp.pad(t, ((0, 0), (1, 0), (0, 0), (0, 0), (0, 0), (0, 0)))[:, :-1]
        return jnp.concatenate([prev, t], axis=2)

    qb = to_blocks(q)
    kk = with_prev(to_blocks(k))
    vv = with_prev(to_blocks(v))
    scores = jnp.einsum('bnqrhe,bnkrhe->bnrhqk', qb, kk).astype(jnp.float32)

    n_idx = jnp.arange(nb)[:, None, None]
    jq = n_idx * ATT_STEPS + jnp.arange(ATT_STEPS)[None, :, None]
    jk = (n_idx - 1) * ATT_STEPS + jnp.arange(2 * ATT_STEPS)[None, None, :]
    steps = jq - jk
    valid = (jk >= 0) & (steps >= 0) & (steps <= ATT_STEPS)
    dist = (steps * dilation).astype(jnp.float32)
    bias = -slopes[None, None, :, None, None] * dist[:, None, None, :, :]
    scores = jnp.where(valid[:, None, None], scores + bias, -jnp.inf)

    lse = jax.nn.logsumexp(scores, axis=-1)
    p = jnp.exp(scores - lse[..., None]).astype(vv.dtype)
    o = jnp.einsum('bnrhqk,bnkrhe->bnqrhe', p, vv)
    o = o.reshape(B, s_pad, H, E)[:, :S]
    lse = lse.transpose(0, 1, 4, 2, 3).reshape(B, s_pad, H)[:, :S]
    return o, lse

def causal_depthwise_conv(u, w, bias):
    out = lax.conv_general_dilated(
        u, w[:, None, :].astype(u.dtype), window_strides=(1,), padding=((CONV_WIDTH - 1, 0),),
        dimension_numbers=('NWC', 'WIO', 'NWC'), feature_group_count=u.shape[-1])
    return out + bias.astype(u.dtype)

def segsum(a):
    cs = jnp.cumsum(a, axis=-1)
    l = a.shape[-1]
    diff = cs[..., :, None] - cs[..., None, :]
    mask = jnp.tril(jnp.ones((l, l), dtype=bool))
    return jnp.where(mask, diff, -jnp.inf)

def ssd_chunked(x, dt, a, b, c):
    Bsz, S, H, P = x.shape
    G, N = b.shape[2], b.shape[3]
    J = H // G
    nc = S // CHUNK
    xg = (x * dt[..., None]).reshape(Bsz, nc, CHUNK, G, J, P)
    adt = (dt * a).reshape(Bsz, nc, CHUNK, G, J).transpose(0, 1, 3, 4, 2)
    bc = b.reshape(Bsz, nc, CHUNK, G, N)
    cc = c.reshape(Bsz, nc, CHUNK, G, N)
    a_cs = jnp.cumsum(adt, axis=-1)

    decay = jnp.exp(segsum(adt))
    cb = jnp.einsum('bclgn,bcsgn->bcgls', cc, bc)
    y_diag = jnp.einsum('bcgjls,bcsgjp->bclgjp', cb[:, :, :, None] * decay, xg)

    decay_to_end = jnp.exp(a_cs[..., -1:] - a_cs).transpose(0, 1, 4, 2, 3)[..., None]
    states = jnp.einsum('bcsgn,bcsgjp->bcgjpn', bc, xg * decay_to_end)

    chunk_decay = jnp.exp(a_cs[..., -1])

    def step(h, inp):
        st, dec = inp
        return h * dec[..., None, None] + st, h

    h0 = jnp.zeros((Bsz, G, J, P, N), dtype=jnp.float32)
    _, prev = lax.scan(step, h0, (jnp.moveaxis(states, 1, 0), jnp.moveaxis(chunk_decay, 1, 0)))
    prev = jnp.moveaxis(prev, 0, 1)

    state_decay = jnp.exp(a_cs).transpose(0, 1, 4, 2, 3)[..., None]
    y_off = jnp.einsum('bclgn,bcgjpn->bclgjp', cc, prev) * state_decay
    return (y_diag + y_off).reshape(Bsz, S, H, P)

def second_inputs(seed: int = 0) -> dict:
    key = jax.random.key(seed)
    ks = jax.random.split(key, 14)
    beta = (8.0 * DEPTH) ** -0.25
    f32 = jnp.float32
    x = jax.random.normal(ks[0], (BATCH, SEQ, D_MODEL), f32)
    col_scale = np.ones((D_IN_PROJ,), np.float32)
    col_scale[2 * D_ATT:3 * D_ATT] = beta
    col_scale[4 * D_ATT + D_SSM:4 * D_ATT + 2 * D_SSM] = beta
    w_in = jax.random.normal(ks[1], (DEPTH, D_MODEL, D_IN_PROJ), f32) * (D_MODEL ** -0.5) * jnp.asarray(col_scale)
    conv_w = jax.random.normal(ks[2], (DEPTH, CONV_WIDTH, D_CONV), f32) * (CONV_WIDTH ** -0.5)
    conv_b = 0.02 * jax.random.normal(ks[3], (DEPTH, D_CONV), f32)
    dt0 = jnp.exp(jax.random.uniform(ks[4], (DEPTH, SSM_HEADS), f32, math.log(1e-3), math.log(1e-1)))
    dt_bias = dt0 + jnp.log(-jnp.expm1(-dt0))
    a_log = jnp.log(jax.random.uniform(ks[5], (DEPTH, SSM_HEADS), f32, 1.0, 16.0))
    d_skip = 1.0 + 0.1 * jax.random.normal(ks[6], (DEPTH, SSM_HEADS), f32)
    att_norm_g = 1.0 + 0.1 * jax.random.normal(ks[7], (DEPTH, D_ATT), f32)
    ssm_norm_g = 1.0 + 0.1 * jax.random.normal(ks[8], (DEPTH, D_SSM), f32)
    w_out = jax.random.normal(ks[9], (DEPTH, D_MIX, D_MODEL), f32) * (D_MIX ** -0.5) * beta
    ln_g = 1.0 + 0.1 * jax.random.normal(ks[10], (DEPTH, D_MODEL), f32)
    ln_b = 0.02 * jax.random.normal(ks[11], (DEPTH, D_MODEL), f32)
    return {'x': x, 'w_in': w_in, 'conv_w': conv_w, 'conv_b': conv_b, 'dt_bias': dt_bias,
            'a_log': a_log, 'd_skip': d_skip, 'att_norm_g': att_norm_g, 'ssm_norm_g': ssm_norm_g,
            'w_out': w_out, 'ln_g': ln_g, 'ln_b': ln_b}

def second_block(x, w_in, conv_w, conv_b, dt_bias, a_log, d_skip, att_norm_g, ssm_norm_g, w_out, ln_g, ln_b):
    alpha = (2.0 * DEPTH) ** 0.25
    slopes = alibi_slopes(ATT_HEADS)
    Bsz, S, _ = x.shape
    for layer in range(DEPTH):
        proj = jnp.einsum('bsd,de->bse', x, w_in[layer])
        q, k, v, z_att, z_ssm, xbc, dt_raw = jnp.split(proj, list(SPLITS), axis=-1)

        q = q.reshape(Bsz, S, ATT_HEADS, ATT_HEAD_DIM) * (ATT_HEAD_DIM ** -0.5)
        k = k.reshape(Bsz, S, ATT_HEADS, ATT_HEAD_DIM)
        v = v.reshape(Bsz, S, ATT_HEADS, ATT_HEAD_DIM)
        o1, l1 = dilated_window_attention(q, k, v, slopes, DILATIONS[0])
        o2, l2 = dilated_window_attention(q, k, v, slopes, DILATIONS[1])
        o3, l3 = dilated_window_attention(q, k, v, slopes, DILATIONS[2])
        wts = jax.nn.softmax(jnp.stack([l1, l2, l3], axis=0), axis=0)
        y_att = (wts[0][..., None] * o1 + wts[1][..., None] * o2 + wts[2][..., None] * o3).astype(x.dtype)
        y_att = rms_norm_2(y_att.reshape(Bsz, S, D_ATT) * jax.nn.silu(z_att), att_norm_g[layer])

        xbc = jax.nn.silu(causal_depthwise_conv(xbc, conv_w[layer], conv_b[layer]))
        xs, bm, cm = jnp.split(xbc, [D_SSM, D_SSM + SSM_GROUPS_2 * SSM_STATE_2], axis=-1)
        dt = jax.nn.softplus(dt_raw.astype(jnp.float32) + dt_bias[layer].astype(jnp.float32))
        a = -jnp.exp(a_log[layer].astype(jnp.float32))
        xs_h = xs.reshape(Bsz, S, SSM_HEADS, SSM_HEAD_DIM).astype(jnp.float32)
        y = ssd_chunked(xs_h, dt, a,
                        bm.reshape(Bsz, S, SSM_GROUPS_2, SSM_STATE_2).astype(jnp.float32),
                        cm.reshape(Bsz, S, SSM_GROUPS_2, SSM_STATE_2).astype(jnp.float32))
        y = y + d_skip[layer].astype(jnp.float32)[:, None] * xs_h
        y_ssm = rms_norm_2(y.reshape(Bsz, S, D_SSM).astype(x.dtype) * jax.nn.silu(z_ssm), ssm_norm_g[layer])

        mix = jnp.concatenate([y_att, y_ssm], axis=-1)
        out = jnp.einsum('bse,ed->bsd', mix, w_out[layer])
        x = layer_norm(alpha * x + out, ln_g[layer], ln_b[layer])
    return x


def setup_inputs(seed=0):
    out = dict(first_inputs(seed))
    for name, value in second_inputs(seed + 1).items():
        if name != "x":
            out[name + "_2"] = value
    return out


def reference(
    x, c, norm_g, w_mod, b_mod, w_in, a_re, a_im, b_re, b_im, c_re, c_im, d_skip, log_dt, w_glu,
    b_glu, w_a_o, w_b_o, w_out, final_g, w_in_2, conv_w_2, conv_b_2, dt_bias_2, a_log_2,
    d_skip_2, att_norm_g_2, ssm_norm_g_2, w_out_2, ln_g_2, ln_b_2,
):
    x = first_block(
        x, c, norm_g, w_mod, b_mod, w_in, a_re, a_im, b_re, b_im, c_re, c_im, d_skip, log_dt,
        w_glu, b_glu, w_a_o, w_b_o, w_out, final_g,
    )
    return second_block(
        x, w_in_2, conv_w_2, conv_b_2, dt_bias_2, a_log_2, d_skip_2, att_norm_g_2, ssm_norm_g_2,
        w_out_2, ln_g_2, ln_b_2,
    )


_drawn_inputs = setup_inputs


def setup_inputs(seed=0):
    import zlib

    import numpy as np

    out = dict(_drawn_inputs(seed))
    spreads = {}
    factors = {'norm_g': 8.0,
     'b_mod': 8.0,
     'a_re': 64.0,
     'a_im': 64.0,
     'b_re': 64.0,
     'b_im': 64.0,
     'c_re': 64.0,
     'c_im': 64.0,
     'log_dt': 64.0,
     'b_glu': 50.274,
     'conv_b_2': 3.46,
     'ln_b_2': 2.676}
    for name, (base, spread) in spreads.items():
        noise = np.random.default_rng([zlib.crc32(name.encode()), seed]).standard_normal(out[name].shape)
        drawn = base * np.exp(spread * noise) if base else spread * noise
        out[name] = __import__('jax').numpy.asarray(drawn.astype(out[name].dtype))
    for name, factor in factors.items():
        out[name] = (out[name] * factor).astype(out[name].dtype)
    return out
```

```python
from contextlib import ExitStack

import numpy as np

import concourse.bass as bass
from concourse import mybir

F32 = mybir.dt.float32
ALU = mybir.AluOpType
ACT = mybir.ActivationFunctionType
AX_X = mybir.AxisListType.X

P = 128
SEQ = 1024
D = 1024
KD = D // P
NT = SEQ // P
LOADW = 4096
BANK = 512

SSM_W = 512
PAIRS = 16
PG = 16
SUB = 4
NCH = SEQ // SUB
BATCH_PAIRS = 4
HEADS1 = 8
DH = 64
TOPK = 256
IDX_SCALE = 512.0 ** -0.5
ATTN_SCALE = 0.125
RMS_EPS = 1e-6
NORM_EPS = 1e-5

HEADS2 = 16
CHUNK = 128
CONV_TILES = 12
ALPHA = 2.0 ** 0.25
SLOPES = [2.0 ** (-8.0 * (h + 1) / HEADS2) for h in range(HEADS2)]

BIG = 1.0e30
CAUSAL_FILL = -1.0e37
TAKEN = -3.0e38
TAKEN_LIMIT = -2.0e38
ROUND = 1.5 * 2.0 ** 23
TWO_PI = 2.0 * np.pi
PI2_A = 6.28125
PI2_B = float(np.float32(0.0019350051879882812))
PI2_C = TWO_PI - PI2_A - PI2_B
SIN_SCALE = 6.2831845
HALF_PI = float(np.float32(np.pi / 2))


def prefix(sizes):
    at, out = 0, {}
    for name, n in sizes:
        out[name] = slice(at, at + n)
        at += n
    return out, at


PARAMS, NPARAM = prefix([
    ("ar", 16), ("ai", 16), ("ldt", 16), ("br", 256), ("bi", 256), ("cr", 256), ("ci", 256),
    ("dskip", 16), ("c", 8), ("normg", 8), ("bshift", 8), ("bscale", 8), ("bglu", 8),
    ("convw", 48), ("convb", 12), ("dtb", 16), ("alog", 16), ("dskip2", 16), ("attg", 8), ("ssmg", 8)])
CONSTS, NCONST = prefix([
    ("ident", 128), ("tri", 128), ("ones", 128), ("step", 256), ("ahead_fill", 128), ("ahead_big", 128)])


def weight_plan():
    loads = ["mod0", "mod1", "mod2", "mod3", "small", "qi", "xa", "za", "glu", "ga0", "ga1", "ao", "q", "zb",
             "gb0", "gb1", "bo", "gate0", "gate1", "out0", "out1", "dt", "xbc0", "xbc1", "xbc2", "zs0", "zs1"]
    loads += [f"pair{j}" for j in range(8)] + [f"wo{j}" for j in range(4)]
    return loads


LOADS = weight_plan()


def unit_plan():
    count = {"small": 6, "glu": 16, "ao": 16, "bo": 16, "dt": 1, "gate0": 1, "gate1": 1}
    for n in range(4):
        count[f"mod{n}"] = 1
        count[f"wo{n}"] = 4
    units, first = [], {}
    for name in LOADS:
        first[name] = len(units)
        units += [(name, i) for i in range(count.get(name, 8))]
    return units, first


UNITS, FIRST = unit_plan()
WIDE_BANKS = 4
PAIR0 = FIRST["pair0"]
PAIR_END = FIRST["wo0"]


def unit_bank(u):
    return u % 2 if PAIR0 <= u < PAIR_END else u % WIDE_BANKS


def bank_before(u):
    for v in range(u - 1, -1, -1):
        if unit_bank(v) == unit_bank(u):
            return v
    return None


def layer_kernel(nc, x, loads, params, consts, rows, alibi, out, x2_dram):
    ctx = ExitStack()
    with ctx:
        def sb(name, shape):
            return ctx.enter_context(nc.sbuf_tensor(name, shape, F32))

        def sem(name):
            return ctx.enter_context(nc.semaphore(name))

        W = sb("W", [P, 2, LOADW])
        hT = sb("hT", [P, KD, SEQ])
        arena = sb("arena", [P, 31744])
        pk = sb("pk", [P, NPARAM])
        ck = sb("ck", [P, NCONST])
        small = sb("small", [P, 2816])
        ps = ctx.enter_context(nc.psum_tensor("ps", [P, 8, BANK], F32))

        def area(a, n, pattern=None, **k):
            v = arena[:, a:a + n]
            return v.rearrange(pattern, **k) if pattern else v

        def par(name):
            return pk[:, PARAMS[name]]

        def con(name):
            return ck[:, CONSTS[name]]

        cursor = [0]

        def little(n, pattern=None, **k):
            v = small[:, cursor[0]:cursor[0] + n]
            cursor[0] += n
            return v.rearrange(pattern, **k) if pattern else v

        ident, tri, ones = con("ident"), con("tri"), con("ones")

        XR0 = area(11776, 8192, "p (t d) -> p t d", t=NT)
        SC = area(0, 4608)
        qiT = area(4608, 4096, "p (f t) -> p f t", f=4)
        yaT = qiT
        qT1 = qiT
        gbT = area(0, 8192, "p (f t) -> p f t", f=KD)
        kiT = area(8704, 1024)
        ytile = area(8704, 1024)
        kT1 = area(9728, 1024)
        vw = area(10752, 1024, "p (t c) -> p t c", t=NT)
        U = area(11776, 4096, "p (g c) -> p g c", g=PAIRS)
        mT = area(11776, 8192, "p (f t) -> p f t", f=KD)
        zaT = area(19968, 4096, "p (f t) -> p f t", f=4)
        ybT = zaT
        zbT = area(24064, 4096, "p (f t) -> p f t", f=4)
        relu_sl = [area(24064 + 1024 * s, 1024) for s in range(2)]
        tmp = [area(28160 + 512 * s, 512) for s in range(4)]
        XR = area(0, 8192, "p (t d) -> p t d", t=NT)
        gate = area(8704, 1024)
        frow = area(9728, 1024)
        bgate = area(24064, 1024)
        BH = area(15872, 1024, "p (r g s q) -> p r g s q", r=2, g=BATCH_PAIRS, s=SUB)
        CE = area(16896, 2048, "p (r g s q) -> p r g s q", r=2, g=BATCH_PAIRS, s=8)
        BT = area(18944, 1024, "p (r g m) -> p r g m", r=2, g=BATCH_PAIRS)
        TP = area(24064, 512, "p (g m) -> p g m", g=BATCH_PAIRS)
        cosT = area(24576, 1024)
        sinT = area(25600, 1024)
        rot_a = area(26624, 1024)
        rot_b = area(27648, 1024)
        Gs = [area(28672 + 1028 * r, 1028, "p (g c) -> p g c", g=BATCH_PAIRS) for r in range(2)]

        Z = area(0, 8192, "p (t d) -> p t d", t=NT)
        xs = area(8192, 8192, "p (t d) -> p t d", t=NT)
        mixS = area(8192, 8192, "p (f t) -> p f t", f=KD)
        BTf = area(16384, 2048, "p (g t) -> p g t", g=2)
        CTf = area(18432, 2048, "p (g t) -> p g t", g=2)
        Btok = area(20480, 2048, "p (t g n) -> p t g n", t=NT, g=2)
        raw = [area(22528 + 1028 * s, 1028) for s in range(2)]
        acc = [area(24584 + 1024 * s, 1024) for s in range(2)]
        cxs = [area(26632 + 1024 * s, 1024) for s in range(2)]
        dif = area(22528, 1024, "p (h l) -> p h l", h=8)
        dif_flat = dif.rearrange("p h l -> p (h l)")
        dec = area(23552, 1024, "p (h l) -> p h l", h=8)
        xg = area(24576, 1024)
        xgd = area(25600, 1024)
        hst = area(26624, 1024)
        cbm = area(27648, 128)
        yt = area(27776, 1024)
        yt2 = area(28800, 512)
        YA = area(0, 8192, "p (t d) -> p t d", t=NT)
        pq = [area(16384 + 4096 * s, 1024) for s in range(2)]
        pkT = [area(17408 + 4096 * s, 1024) for s in range(2)]
        pv_ = [area(18432 + 4096 * s, 1024, "p (t c) -> p t c", t=NT) for s in range(2)]
        pz = [area(19456 + 4096 * s, 1024, "p (t c) -> p t c", t=NT) for s in range(2)]
        mixA = area(16384, 8192, "p (f t) -> p f t", f=KD)
        TB = [area(24576 + 1024 * s, 1024) for s in range(2)]
        dist = area(29696, 1024)
        nlog = area(30720, 1024)
        res = area(0, 8192, "p (t d) -> p t d", t=NT)
        lng = area(24576, 1024)
        lnb = area(25600, 1024)
        at1 = dict(sbuf=[area(28160 + 1024 * s, 1024) for s in range(2)],
                   pt=[area(30208 + 512 * s, 512) for s in range(2)])
        at2 = dict(sbuf=[area(26624 + 1024 * s, 1024) for s in range(2)],
                   pt=[area(28672 + 512 * s, 512) for s in range(2)])
        zt = little(1024)

        ss = little(8)
        rs = little(8)
        csil = little(8)
        sc1 = little(8)
        shf = little(8)
        gam = little(8)
        half_pi = little(1)
        dts, ard, aid, kk, th, r1, r2 = (little(16) for _ in range(7))
        pw = little(160, "p (r k g) -> p r k g", r=2, k=5)
        coef = little(32, "p (r g) -> p r g", r=2)
        frac = little(16)
        rho = little(16)
        mx = little(8)
        mneg4 = little(4)
        den = little(128)
        rden = little(16)
        modv = little(16)
        dtr, dtv, adt, cst, ecs, dte, ctot = (little(128) for _ in range(7))
        aexp = little(16)
        nmu = little(8)

        s_w = [sem(f"weights_loaded{i}") for i in range(2)]
        s_par = sem("params_loaded")
        s_x = sem("x_loaded")
        s_unit = sem("unit_multiplied")
        s_free = sem("unit_evacuated")
        s_v = sem("vector_step")
        s_a = sem("scalar_step")
        s_g = sem("gpsimd_step")
        s_csil = sem("silu_c_ready")
        s_ssq = sem("squares_summed")
        s_mean = sem("mean_square_ready")
        s_root = sem("root_ready")
        s_xn = sem("tile_normalised")
        s_xt = sem("tile_transposed")
        s_mod = sem("scale_shift_ready")
        s_ht = sem("hT_written")
        s_ixs = sem("index_product")
        s_ixr = sem("index_relu")
        s_ixa = sem("index_added")
        s_mask = sem("masks_ready")
        s_prm = sem("state_params_scalar")
        s_prv = sem("state_params_vector")
        s_bh = sem("input_blocks_placed")
        s_bhg = sem("output_blocks_placed")
        s_stm = sem("state_matrices_made")
        s_ste = sem("state_matrices_copied")
        s_turn = sem("turns_reduced")
        s_trig = sem("rotations_ready")
        s_zin = sem("state_inputs_made")
        s_hout = sem("states_ready")
        s_yps = sem("state_outputs_made")
        s_ysm = sem("state_outputs_added")
        s_ya = sem("gelu_placed")
        s_comb = sem("unit_combined")
        s_row = sem("rows_loaded")
        s_xr = sem("residual_loaded")
        s_gate = sem("gate_ready")
        s_x2 = sem("second_input_ready")
        s_x2st = sem("second_input_stored")
        s_xt2 = sem("second_transposed")
        s_ht2 = sem("second_hT_written")
        s_dtv = sem("dt_vector")
        s_dta = sem("dt_scalar")
        s_conv = sem("channels_convolved")
        s_silu = sem("channels_activated")
        s_ct = sem("channels_transposed")
        s_xs = sem("channels_placed")
        s_cum = sem("decay_sums_made")
        s_cume = sem("decay_sums_copied")
        s_csb = sem("decay_rows_made")
        s_dif = sem("decay_rows_read")
        s_xg = sem("scaled_inputs_ready")
        s_dec = sem("decays_ready")
        s_mt = sem("masked_products_ready")
        s_yd = sem("chunk_outputs_made")
        s_yo = sem("chunk_outputs_read")
        s_st = sem("state_zeroed")
        s_nrm = {n: [sem(f"{n}_{w}") for w in ("squares", "mean", "root", "scaled", "transposed", "placed")]
                 for n in ("ssm", "att")}
        s_alibi = sem("alibi_loaded")
        s_zs = sem("pair_gate_ready")
        s_ln = [sem(f"layernorm_{w}") for w in ("sum", "mean", "squares", "var", "root", "row")]
        s_out = sem("output_stored")
        s_att = [{w: sem(f"att{b}_{w}") for w in ("scores", "biased", "exp", "transposed", "copied", "weighted",
                                                  "read", "yT", "yT_used")} for b in (1, 2)]
        block = ctx.enter_context(nc.Block())

        def unit_end(name):
            n = LOADS.index(name)
            return FIRST[LOADS[n + 1]] if n + 1 < len(LOADS) else len(UNITS)

        def sc_at(i):
            return SC[:, 64 * i * (i + 1):64 * i * (i + 1) + P * (i + 1)]

        items1 = [(i, h, i, h) for i in range(NT) for h in range(HEADS1)]
        items2 = [(h, i, i, h) for h in range(HEADS2) for i in range(NT)]

        def groups_of(items):
            n, out_ = 0, []
            for it in items:
                blocks, mine = it[2] + 1, []
                for b in range(0, blocks, 4):
                    mine.append((n, b, min(4, blocks - b)))
                    n += 1
                out_.append(mine)
            return out_

        groups1, groups2 = groups_of(items1), groups_of(items2)
        PAIR_UNIT_STEPS = range(0, 16, 2)

        @block.sync
        def _(sp):
            def load(n):
                if n >= 2:
                    sp.wait_ge(s_unit, unit_end(LOADS[n - 2]))
                nc.sync.dma_start(W[:, n % 2, :], loads[n]).then_inc(s_w[n % 2], 16)

            nc.sync.dma_start(pk[:], params).then_inc(s_par, 16)
            load(0)
            nc.sync.dma_start(XR0[:, 0:4, :], x[0:512].rearrange("(t p) d -> p t d", p=P)).then_inc(s_x, 16)
            nc.sync.dma_start(XR0[:, 4:8, :], x[512:1024].rearrange("(t p) d -> p t d", p=P)).then_inc(s_x, 16)
            nc.sync.dma_start(ck[:], consts).then_inc(s_par, 16)
            for n in range(1, len(LOADS)):
                load(n)

        @block.gpsimd
        def _(pool):
            chain = [0]

            def link(ins):
                chain[0] += 1
                ins.then_inc(s_g, 1)
                pool.wait_ge(s_g, chain[0])

            def mult(o, a, b):
                return nc.gpsimd.tensor_tensor(o, a, b, ALU.mult)

            pool.wait_ge(s_prv, 3)
            pool.wait_ge(s_ht, 16)
            link(nc.gpsimd.memset(CE[:], 0.0))
            pool.wait_ge(s_ixa, 6 * HEADS1)
            for b in range(4):
                gs = slice(BATCH_PAIRS * b, BATCH_PAIRS * (b + 1))
                t1, t2 = (area(31368 + 64 * n, 64, "p (g q) -> p g q", g=BATCH_PAIRS) for n in range(2))
                cr = par("cr").rearrange("p (g q) -> p g q", g=PAIRS)[:, gs, :]
                ci = par("ci").rearrange("p (g q) -> p g q", g=PAIRS)[:, gs, :]
                if b:
                    pool.wait_ge(s_yps, b)
                for k in range(5):
                    er = pw[:, 0, k, gs].unsqueeze(2).to_broadcast([P, BATCH_PAIRS, PG])
                    ei = pw[:, 1, k, gs].unsqueeze(2).to_broadcast([P, BATCH_PAIRS, PG])
                    mult(t1, cr, er)
                    link(mult(t2, ci, ei))
                    for half in range(2):
                        rows_, cols = slice(64 * half, 64 * half + 64), slice(PG * half, PG * half + PG)
                        last = nc.gpsimd.tensor_tensor(CE[rows_, 0, :, 3 + k, cols], t1[rows_], t2[rows_], ALU.subtract)
                    link(last)
                    link(nc.gpsimd.tensor_scalar(t1, cr, -1.0, None, ALU.mult))
                    link(mult(t1, t1, ei))
                    link(mult(t2, ci, er))
                    for half in range(2):
                        rows_, cols = slice(64 * half, 64 * half + 64), slice(PG * half, PG * half + PG)
                        last = nc.gpsimd.tensor_tensor(CE[rows_, 1, :, 3 + k, cols], t1[rows_], t2[rows_], ALU.subtract)
                        if k == 4:
                            last.then_inc(s_bhg, 1)
                        elif half:
                            link(last)
                pool.wait_ge(s_bhg, 2 * (b + 1))
                if b:
                    pool.wait_ge(s_hout, b)
                turn = cosT.rearrange("p (g c) -> p g c", g=BATCH_PAIRS)
                link(mult(turn, con("step").unsqueeze(1).to_broadcast([P, BATCH_PAIRS, NCH]),
                          frac[:, gs].unsqueeze(2).to_broadcast([P, BATCH_PAIRS, NCH])))
                link(nc.gpsimd.tensor_scalar(sinT, cosT, ROUND, None, ALU.add))
                link(nc.gpsimd.tensor_scalar(sinT, sinT, ROUND, None, ALU.subtract))
                nc.gpsimd.tensor_tensor(sinT, cosT, sinT, ALU.subtract).then_inc(s_turn, 1)
                pool.wait_ge(s_turn, b + 1)

            for c in range(8):
                ct, half = c // 2, c % 2
                za = zaT[:, ct, half * 512:half * 512 + 512]
                a, s = tmp[(2 * c) % 4], tmp[(2 * c + 1) % 4]
                pool.wait_ge(s_free, FIRST["glu"] + 2 * c + 2)
                link(mult(a, a, za))
                mult(za, a, s).then_inc(s_comb, 1)
                pool.wait_ge(s_comb, c + 1)
            for i in range(16):
                pool.wait_ge(s_free, FIRST["ao"] + i + 1)
                m = mT[:, i // 2, (i % 2) * 512:(i % 2) * 512 + 512]
                mult(m, m, tmp[i % 4]).then_inc(s_comb, 1)
                pool.wait_ge(s_comb, 9 + i)
            for i in range(16):
                pool.wait_ge(s_free, FIRST["bo"] + i + 1)
                cols = slice((i % 2) * 512, (i % 2) * 512 + 512)
                link(mult(tmp[i % 4], tmp[i % 4], gbT[:, i // 2, cols]))
                nc.gpsimd.tensor_tensor(mT[:, i // 2, cols], mT[:, i // 2, cols], tmp[i % 4], ALU.add).then_inc(s_comb, 1)
                pool.wait_ge(s_comb, 25 + i)
            pool.wait_ge(s_comb, 40)
            nc.gpsimd.dma_start(XR[:], x.rearrange("(t p) d -> p t d", p=P)).then_inc(s_xr, 16)
            pool.wait_ge(s_att[0]["scores"], 64)
            pool.wait_ge(s_att[0]["yT"], NT)
            pool.wait_ge(s_att[0]["yT_used"], NT)
            nc.gpsimd.dma_start(bgate, rows[0]).then_inc(s_row, 16)
            nc.gpsimd.dma_start(frow, rows[1]).then_inc(s_row, 16)
            pool.wait_ge(s_gate, 1)
            pool.wait_ge(s_xr, 16)
            for i in range(16):
                pool.wait_ge(s_free, FIRST["out0"] + i + 1)
                cols = slice((i // 8) * 512, (i // 8) * 512 + 512)
                link(mult(tmp[i % 4], tmp[i % 4], gate[:, cols]))
                nc.gpsimd.tensor_tensor(XR[:, i % 8, cols], XR[:, i % 8, cols], tmp[i % 4], ALU.add).then_inc(s_comb, 1)
                pool.wait_ge(s_comb, 41 + i)
            nc.gpsimd.dma_start(dist, alibi[0]).then_inc(s_alibi, 16)
            nc.gpsimd.dma_start(nlog, alibi[1]).then_inc(s_alibi, 16)
            for t in range(NT):
                pool.wait_ge(s_x2, t + 1)
                nc.gpsimd.dma_start(x2_dram[t], XR[:, t, :]).then_inc(s_x2st, 16)
            for m in range(16):
                pool.wait_ge(s_dec, m + 1)
                pool.wait_ge(s_dif, m + 1)
                mult(dec, dec, cbm.unsqueeze(1).to_broadcast([P, 8, CHUNK])).then_inc(s_mt, 1)
                pool.wait_ge(s_mt, m + 1)
            for j in range(8):
                pool.wait_ge(s_free, FIRST[f"pair{j}"] + 8)
                z_ = pz[j % 2].rearrange("p t c -> p (t c)")
                link(mult(zt, zt, z_))
                nc.gpsimd.tensor_tensor(z_, z_, zt, ALU.add).then_inc(s_zs, 1)
                pool.wait_ge(s_zs, j + 1)
            pool.wait_ge(s_nrm["att"][4], 16)
            pool.wait_ge(s_x2st, 16 * NT)
            nc.gpsimd.dma_start(res[:], x2_dram.rearrange("t p d -> p t d")).then_inc(s_xr, 16)
            nc.gpsimd.dma_start(lng, rows[2]).then_inc(s_row, 16)
            nc.gpsimd.dma_start(lnb, rows[3]).then_inc(s_row, 16)
            for t in range(NT):
                pool.wait_ge(s_ln[5], t + 1)
                nc.gpsimd.dma_start(out[t * P:(t + 1) * P, :], res[:, t, :]).then_inc(s_out, 16)
            pool.wait_ge(s_out, 16 * NT)

        @block.tensor
        def _(pe):
            mm = nc.tensor.matmul

            def operands(name, i):
                w = W[:, LOADS.index(name) % 2, :]
                w8 = w.rearrange("p (k n) -> p k n", k=KD)
                w4 = w.rearrange("p (k n) -> p k n", k=4)
                half = (i % 2) * 512
                if name[:3] == "mod":
                    return KD, [(slice(ct, ct + 1), lambda k, ct=ct: w8[:, k, ct * P:(ct + 1) * P],
                                 lambda k: csil[:, k:k + 1]) for ct in range(4)]
                if name[:4] == "gate":
                    return KD, [(slice(0, 512), lambda k: csil[:, k:k + 1].to_broadcast([P, P]), lambda k: w8[:, k, :])]
                if name == "small" and i < 4:
                    return KD, [(slice(0, 512), lambda k: w8[:, k, (i // 2) * P:(i // 2) * P + P],
                                 lambda k: hT[:, k, half:half + 512])]
                if name == "small":
                    return KD, [(slice(j * P, j * P + 72),
                                 lambda k, t=4 * (i - 4) + j: hT[:, k, t * P:(t + 1) * P],
                                 lambda k: w8[:, k, 256:328]) for j in range(4)]
                if name == "xa":
                    perm = [hT[:, k, :].rearrange("p (c s) -> p s c", s=SUB)[:, 2 * (i % 2):2 * (i % 2) + 2, :]
                            for k in range(KD)]
                    return KD, [(slice(0, 512), lambda k: w8[:, k, (i // 2) * P:(i // 2) * P + P], lambda k: perm[k])]
                if name in ("qi", "q", "zb", "za", "ga0", "ga1", "gb0", "gb1", "xbc0", "xbc1", "xbc2"):
                    return KD, [(slice(0, 512), lambda k: w8[:, k, (i // 2) * P:(i // 2) * P + P],
                                 lambda k: hT[:, k, half:half + 512])]
                if name == "glu":
                    c0 = (i % 2) * 512 + (i // 4) * P
                    h0 = ((i // 2) % 2) * 512
                    return 4, [(slice(0, 512), lambda k: w4[:, k, c0:c0 + P], lambda k: yaT[:, k, h0:h0 + 512])]
                if name in ("ao", "bo"):
                    src = zaT if name == "ao" else ybT
                    return 4, [(slice(0, 512), lambda k: w4[:, k, (i // 2) * P:(i // 2) * P + P],
                                lambda k: src[:, k, half:half + 512])]
                if name in ("out0", "out1"):
                    return KD, [(slice(0, 512), lambda k: mT[:, k, i * P:(i + 1) * P], lambda k: w8[:, k, :])]
                if name in ("zs0", "zs1"):
                    return KD, [(slice(0, 512), lambda k: hT[:, k, i * P:(i + 1) * P], lambda k: w8[:, k, :])]
                if name == "dt":
                    return KD, [(slice(t * 16, t * 16 + 16), lambda k, t=t: hT[:, k, t * P:(t + 1) * P],
                                 lambda k: w8[:, k, 0:16]) for t in range(NT)]
                if name[:4] == "pair" and i < 4:
                    return KD, [(slice(0, 512), lambda k: w8[:, k, (i // 2) * P:(i // 2) * P + P],
                                 lambda k: hT[:, k, half:half + 512])]
                if name[:4] == "pair":
                    c0 = (i // 2) * P
                    return KD, [(slice(j * P, j * P + P), lambda k, t=4 * (i % 2) + j: hT[:, k, t * P:(t + 1) * P],
                                 lambda k: w8[:, k, c0:c0 + P]) for j in range(4)]
                w16 = w.rearrange("p (k n) -> p k n", k=16)
                return 16, [(slice(j * 256, j * 256 + 256),
                             lambda k, t=2 * i + j: (mixA if k < 8 else mixS)[:, k % 8, t * P:(t + 1) * P],
                             lambda k: w16[:, k, :]) for j in range(2)]

            def unit(u):
                name, i = UNITS[u]
                n = LOADS.index(name)
                if i == 0:
                    pe.wait_ge(s_w[n % 2], 16 * (n // 2 + 1))
                before = bank_before(u)
                if before is not None:
                    pe.wait_ge(s_free, before + 1)
                steps, pieces = operands(name, i)
                for cols, lhs, rhs in pieces:
                    for k in range(steps):
                        o = ps[:, unit_bank(u), cols]
                        r = rhs(k)
                        if len(r.shape) == 3:
                            o = o.rearrange("p (a b) -> p a b", a=r.shape[1])
                        last = mm(o, lhs(k), r, start=(k == 0), stop=(k == steps - 1))
                last.then_inc(s_unit, 1)

            def units(name):
                for u in range(FIRST[name], unit_end(name)):
                    unit(u)

            def turn_tiles(src, made, read, count0=0):
                for n in range(16):
                    k, half = n // 2, n % 2
                    if n >= 4:
                        pe.wait_ge(read, n - 3)
                    for j in range(4):
                        last = nc.tensor.transpose(ps[:, 4 + n % 4, j * P:(j + 1) * P],
                                                   src[:, 4 * half + j, k * P:(k + 1) * P], ident)
                    last.then_inc(made, 1)

            def attention(sems, items, groups, q_of, k_of, v_of, tiles, extra=None):
                pending = None

                def weigh(pend):
                    n, g, b0, nb = pend
                    outer, inner, i, _ = items[n]
                    pe.wait_ge(sems["copied"], g + 1)
                    if b0 == 0 and inner == 0 and outer >= 2:
                        pe.wait_ge(sems["read"], outer - 1)
                    pt = tiles["pt"][g % 2]
                    for j in range(nb):
                        last = mm(ps[:, 6 + outer % 2, inner * DH:(inner + 1) * DH], pt[:, j * P:(j + 1) * P],
                                  v_of(items[n], b0 + j), start=(b0 + j == 0), stop=(b0 + j == i))
                    last.then_inc(sems["weighted"], 1)

                for n in range(len(items) + 1):
                    if n < len(items):
                        i = items[n][2]
                        if n >= 1:
                            pe.wait_ge(sems["biased"], n)
                        q, k = q_of(items[n]), k_of(items[n])
                        keys = P * (i + 1)
                        for a in range(0, keys, BANK):
                            e = min(a + BANK, keys)
                            last = mm(ps[:, 2 + a // BANK, 0:e - a], q, k[:, a:e], start=True, stop=True)
                        last.then_inc(sems["scores"], 1)
                    if n >= 1:
                        pe.wait_ge(sems["exp"], n)
                        for g, b0, nb in groups[n - 1]:
                            if g >= 2:
                                pe.wait_ge(sems["copied"], g - 1)
                            for j in range(nb):
                                last = nc.tensor.transpose(ps[:, 4 + g % 2, j * P:(j + 1) * P],
                                                           tiles["sbuf"][(n - 1) % 2][:, (b0 + j) * P:(b0 + j + 1) * P],
                                                           ident)
                            last.then_inc(sems["transposed"], 1)
                            if pending is not None:
                                weigh(pending)
                            pending = (n - 1, g, b0, nb)
                    if extra is not None:
                        extra(n)
                weigh(pending)

            pe.wait_ge(s_par, 32)
            pe.wait_ge(s_csil, 1)
            for n in range(4):
                units(f"mod{n}")
            pe.wait_ge(s_xn, NT)
            turn_tiles(XR0, s_xt, s_ht)
            pe.wait_ge(s_ht, 16)
            units("small")
            units("qi")
            units("xa")
            pe.wait_ge(s_free, unit_end("qi"))
            n = 0
            for i in range(2, NT):
                for h in range(HEADS1):
                    if n >= 2:
                        pe.wait_ge(s_ixr, n - 1)
                    rows_ = slice(64 * (h % 2), 64 * (h % 2) + 64)
                    keys = P * (i + 1)
                    for a in range(0, keys, BANK):
                        e = min(a + BANK, keys)
                        last = mm(ps[:, 4 + 2 * (n % 2) + a // BANK, 0:e - a], qiT[rows_, h // 2, i * P:(i + 1) * P],
                                  kiT[rows_, a:e], start=True, stop=True)
                    last.then_inc(s_ixs, 1)
                    n += 1
            pe.wait_ge(s_ixr, n)
            pe.wait_ge(s_free, unit_end("xa"))
            for b in range(4):
                pe.wait_ge(s_bh, b + 1)
                pe.wait_ge(s_bhg, 2 * (b + 1))
                if b:
                    pe.wait_ge(s_ysm, b)
                for r in range(2):
                    for g in range(BATCH_PAIRS):
                        nc.tensor.transpose(ps[:, 4 + r, g * P:(g + 1) * P],
                                            BH[:, r, g].rearrange("p s q -> p (s q)"), ident)
                for g in range(BATCH_PAIRS):
                    for s in range(SUB):
                        for r in range(2):
                            last = mm(ps[32 * s:32 * s + 32, 6, g * P:(g + 1) * P], BH[:, r, g, 3, :],
                                      CE[:, r, g, 3 - s:7 - s, :].rearrange("p s q -> p (s q)"),
                                      start=(r == 0), stop=(r == 1))
                last.then_inc(s_stm, 1)
                for u in range(FIRST["za"] + 2 * b, FIRST["za"] + 2 * b + 2):
                    unit(u)
                pe.wait_ge(s_ste, b + 1)
                for r in range(2):
                    for g in range(BATCH_PAIRS):
                        last = mm(ps[:, 4 + 2 * r + g // 2, (g % 2) * NCH:(g % 2 + 1) * NCH], BT[:, r, g, :],
                                  U[:, BATCH_PAIRS * b + g, :], start=True, stop=True)
                last.then_inc(s_zin, 1)
                pe.wait_ge(s_hout, b + 1)
                for g in range(BATCH_PAIRS):
                    o = ps[:, 4 + g // 2, (g % 2) * NCH:(g % 2 + 1) * NCH]
                    mm(o, TP[:, g, :], U[:, BATCH_PAIRS * b + g, :], start=True, stop=False)
                    for r in range(2):
                        last = mm(o, CE[:, r, g, 4:8, :].rearrange("p s q -> p (s q)"), Gs[r][:, g, 0:NCH],
                                  start=False, stop=(r == 1))
                last.then_inc(s_yps, 1)
            pe.wait_ge(s_ya, 4)
            units("glu")
            units("ga0")
            units("ga1")
            pe.wait_ge(s_comb, 8)
            units("ao")
            units("q")
            units("zb")
            pe.wait_ge(s_free, unit_end("zb"))
            pe.wait_ge(s_ysm, 4)

            def y_turn(n):
                if n >= 10 and (n - 10) % 8 == 0 or n == 65:
                    i = min((n - 10) // 8, 7) if n != 65 else 7
                    pe.wait_ge(s_att[0]["read"], i + 1)
                    if i >= 2:
                        pe.wait_ge(s_att[0]["yT_used"], i - 1)
                    for j in range(4):
                        last = nc.tensor.transpose(ps[:, i % 2, j * P:(j + 1) * P],
                                                   ytile[:, (i % 2) * 512 + j * P:(i % 2) * 512 + (j + 1) * P], ident)
                    last.then_inc(s_att[0]["yT"], 1)

            def rows_of(h):
                return slice(64 * (h % 2), 64 * (h % 2) + 64)

            attention(s_att[0], items1, groups1,
                      lambda it: qT1[rows_of(it[3]), it[3] // 2, it[2] * P:(it[2] + 1) * P],
                      lambda it: kT1[rows_of(it[3]), :],
                      lambda it, b: vw[:, b, 0:DH], at1, y_turn)
            y_turn(65)
            pe.wait_ge(s_att[0]["yT_used"], 8)
            units("gb0")
            units("gb1")
            units("bo")
            units("gate0")
            units("gate1")
            pe.wait_ge(s_comb, 40)
            units("out0")
            units("out1")

            pe.wait_ge(s_x2, NT)
            turn_tiles(XR, s_xt2, s_ht2)
            pe.wait_ge(s_ht2, 16)
            units("dt")

            def turn_channels(ct):
                pe.wait_ge(s_silu, ct + 1)
                src = cxs[ct % 2] if ct < 8 else BTf[:, ct - 8, :]
                if ct >= 2:
                    pe.wait_ge(s_xs, ct - 1)
                for t in range(NT):
                    last = nc.tensor.transpose(ps[:, 4 + 2 * (ct % 2) + t // 4, (t % 4) * P:(t % 4 + 1) * P],
                                               src[:, t * P:(t + 1) * P], ident)
                last.then_inc(s_ct, 1)

            for ct in range(CONV_TILES):
                for half in range(2):
                    unit(FIRST["xbc0"] + 2 * ct + half)
                if 2 <= ct < 12:
                    turn_channels(ct - 2)
            units("zs0")
            units("zs1")
            pe.wait_ge(s_dtv, 3)
            pe.wait_ge(s_xs, 10)
            mm(ps[:, 6, 0:128], tri, adt, start=True, stop=True)
            mm(ps[:, 6, 128:256], ones, adt, start=True, stop=True).then_inc(s_cum, 1)

            def decay_rows(m):
                c, g = m // 2, m % 2
                if m:
                    pe.wait_ge(s_dif, m)
                for h in range(8):
                    a = adt[:, c * 16 + g * 8 + h:c * 16 + g * 8 + h + 1].to_broadcast([P, P])
                    mm(ps[:, h // 4, (h % 4) * P:(h % 4 + 1) * P], a, tri, start=True, stop=True)
                mm(ps[:, 2, 0:P], BTf[:, g, c * P:(c + 1) * P], CTf[:, g, c * P:(c + 1) * P], start=True,
                   stop=True).then_inc(s_csb, 1)

            pe.wait_ge(s_free, unit_end("zs1"))
            pe.wait_ge(s_silu, 12)
            pe.wait_ge(s_st, 1)
            decay_rows(0)
            for m in range(16):
                c, g = m // 2, m % 2
                if m + 1 < 16:
                    decay_rows(m + 1)
                pe.wait_ge(s_mt, m + 1)
                pe.wait_ge(s_xg, m + 1)
                if m:
                    pe.wait_ge(s_yo, m)
                for h in range(8):
                    mm(ps[:, 3, h * DH:(h + 1) * DH], dec[:, h, :], xg[:, h * DH:(h + 1) * DH], start=True, stop=True)
                mm(ps[:, 4, :], CTf[:, g, c * P:(c + 1) * P], hst[:, g * 512:g * 512 + 512], start=True, stop=True)
                mm(ps[:, 5, :], Btok[:, c, g, :], xgd[:, 0:512], start=True, stop=True).then_inc(s_yd, 1)
            pe.wait_ge(s_yo, 16)
            pe.wait_ge(s_nrm["ssm"][3], NT)
            turn_tiles(Z, s_nrm["ssm"][4], s_nrm["ssm"][5])
            pe.wait_ge(s_nrm["ssm"][5], 16)
            units("pair0")

            def next_pair(n):
                j, step = n // 16 + 1, n % 16
                if j < 8 and step in PAIR_UNIT_STEPS:
                    unit(FIRST[f"pair{j}"] + PAIR_UNIT_STEPS.index(step))

            pe.wait_ge(s_free, unit_end("pair0"))
            attention(s_att[1], items2, groups2,
                      lambda it: pq[(it[3] // 2) % 2][rows_of(it[3]), it[2] * P:(it[2] + 1) * P],
                      lambda it: pkT[(it[3] // 2) % 2][rows_of(it[3]), :],
                      lambda it, b: pv_[(it[3] // 2) % 2][:, b, DH * (it[3] % 2):DH * (it[3] % 2) + DH],
                      at2, next_pair)
            pe.wait_ge(s_nrm["att"][3], NT)
            turn_tiles(YA, s_nrm["att"][4], s_nrm["att"][5])
            pe.wait_ge(s_nrm["att"][5], 16)
            for j in range(4):
                units(f"wo{j}")

        @block.scalar
        def _(act):
            A = nc.scalar.activation
            chain = [0]

            def link(ins):
                chain[0] += 1
                ins.then_inc(s_a, 1)
                act.wait_ge(s_a, chain[0])

            def evac(u):
                name, i = UNITS[u]
                act.wait_ge(s_unit, u + 1)
                bank = ps[:, unit_bank(u), :]
                half = slice((i % 2) * 512, (i % 2) * 512 + 512)
                if name[:3] == "mod":
                    n = int(name[3])
                    last = A(modv[:, 4 * n:4 * n + 4], bank[:, 0:4], ACT.Copy)
                elif name == "small" and i < 4:
                    last = A((kT1 if i < 2 else kiT)[:, half], bank, ACT.Copy)
                elif name == "small":
                    last = A(vw[:, 4 * (i - 4):4 * (i - 3), 0:72],
                             bank.rearrange("p (t c) -> p t c", t=4)[:, :, 0:72], ACT.Copy)
                elif name == "qi":
                    last = A(qiT[:, i // 2, half], bank, ACT.Copy)
                elif name == "xa":
                    for s in range(2):
                        for j in range(4):
                            r0 = 32 * (2 * (i % 2) + s)
                            last = A(U[r0:r0 + 32, 4 * (i // 2) + j, :],
                                     ps[32 * j:32 * j + 32, unit_bank(u), s * NCH:(s + 1) * NCH], ACT.Copy)
                elif name in ("za", "zb"):
                    last = A((zaT if name == "za" else zbT)[:, i // 2, half], bank, ACT.Silu)
                elif name == "glu":
                    w = i
                    if w >= 4:
                        act.wait_ge(s_comb, (w - 4) // 2 + 1)
                    ct = i // 4
                    b = par("bglu")[:, 4 * (i % 2) + ct:4 * (i % 2) + ct + 1]
                    last = A(tmp[w % 4], bank, ACT.Sigmoid if i % 2 else ACT.Identity, bias=b)
                elif name in ("ga0", "ga1"):
                    last = A(mT[:, 4 * int(name[2]) + i // 2, half], bank, ACT.Sigmoid)
                elif name in ("gb0", "gb1"):
                    last = A(gbT[:, 4 * int(name[2]) + i // 2, half], bank, ACT.Sigmoid)
                elif name in ("ao", "bo", "out0", "out1"):
                    c = {"ao": 8, "bo": 24, "out0": 40, "out1": 48}[name] + i
                    act.wait_ge(s_comb, max(c - 3, 8))
                    last = A(tmp[i % 4], bank, ACT.Copy)
                elif name == "q":
                    last = A(qT1[:, i // 2, half], bank, ACT.Copy, scale=-ATTN_SCALE)
                elif name[:4] == "gate":
                    r = int(name[4])
                    last = A(gate[:, 512 * r:512 * r + 512], bank, ACT.Copy)
                elif name == "dt":
                    last = A(dtr, bank[:, 0:128], ACT.Copy)
                elif name[:3] == "xbc":
                    ct = 4 * int(name[3]) + i // 2
                    if ct >= 2:
                        act.wait_ge(s_conv, ct - 1)
                    last = A(raw[ct % 2][:, 3 + (i % 2) * 512:3 + (i % 2) * 512 + 512], bank, ACT.Copy)
                elif name in ("zs0", "zs1"):
                    last = A(Z[:, i, int(name[2]) * 512:int(name[2]) * 512 + 512], bank, ACT.Silu)
                elif name[:4] == "pair":
                    j = int(name[4])
                    if i == 0 and j >= 2:
                        act.wait_ge(s_att[1]["read"], 2 * (j - 1))
                    if i == 6 and j >= 1:
                        act.wait_ge(s_zs, j)
                    if i < 2:
                        last = A(pq[j % 2][:, half], bank, ACT.Copy, scale=-ATTN_SCALE)
                    elif i < 4:
                        last = A(pkT[j % 2][:, half], bank, ACT.Copy)
                    else:
                        b4 = bank.rearrange("p (t c) -> p t c", t=4)
                        ts_ = slice(4 * (i % 2), 4 * (i % 2) + 4)
                        if i < 6:
                            last = A(pv_[j % 2][:, ts_, :], b4, ACT.Copy)
                        else:
                            A(zt[:, half], bank, ACT.Tanh, scale=0.5)
                            last = A(pz[j % 2][:, ts_, :], b4, ACT.Copy, scale=0.5)
                last.then_inc(s_free, 1)

            def evacs(name):
                for u in range(FIRST[name], unit_end(name)):
                    evac(u)

            def squares(src, sem_, junk):
                for t in range(NT):
                    last = A(junk(t), src[:, t, :], ACT.Square, accum_out=ss[:, t:t + 1])
                    if t < NT - 1 and junk(t) is junk(t + 1):
                        link(last)
                last.then_inc(sem_, 1)

            def attention(sems, items, groups, tiles, extra=None):
                for n in range(len(items) + 1):
                    if n < len(items):
                        keys = P * (items[n][2] + 1)
                        act.wait_ge(sems["biased"], n + 1)
                        t = tiles["sbuf"][n % 2][:, 0:keys]
                        outer, inner = items[n][0], items[n][1]
                        if outer >= 2 and inner == 0:
                            act.wait_ge(sems["read"], outer - 1)
                        A(t, t, ACT.Exp, bias=mneg4[:, n % 4:n % 4 + 1], scale=-1.0,
                          accum_out=den[:, (outer % 2) * 8 + inner:(outer % 2) * 8 + inner + 1]).then_inc(sems["exp"], 1)
                    if extra is not None:
                        extra(n)

            act.wait_ge(s_par, 32)
            A(csil, par("c"), ACT.Silu).then_inc(s_csil, 1)
            act.wait_ge(s_x, 32)
            squares(XR0, s_ssq, lambda t: hT[:, t, :])
            act.wait_ge(s_mean, 1)
            A(rs, rs, ACT.Sqrt).then_inc(s_root, 1)
            A(dts, par("ldt"), ACT.Exp).then_inc(s_prm, 1)
            for n in range(4):
                evacs(f"mod{n}")
            evacs("small")
            evacs("qi")
            act.wait_ge(s_prv, 1)
            A(r1, ard, ACT.Exp)
            A(rho, ard, ACT.Exp, scale=4.0).then_inc(s_prm, 1)
            A(th, th, ACT.Sin)
            A(r2, r2, ACT.Sin, scale=-1.0, bias=half_pi).then_inc(s_prm, 1)
            evacs("xa")
            for n in range(6 * HEADS1):
                keys = P * (2 + n // HEADS1 + 1)
                act.wait_ge(s_ixs, n + 1)
                if n >= 2:
                    act.wait_ge(s_ixa, n - 1)
                b = 4 + 2 * (n % 2)
                A(relu_sl[n % 2][:, 0:keys], ps[:, b:b + 2, :].rearrange("p a b -> p (a b)")[:, 0:keys], ACT.Relu,
                  scale=IDX_SCALE).then_inc(s_ixr, 1)
            for b in range(4):
                act.wait_ge(s_turn, b + 1)
                link(A(cosT, sinT, ACT.Abs))
                A(cosT, cosT, ACT.Sin, scale=-SIN_SCALE, bias=half_pi)
                A(sinT, sinT, ACT.Sin, scale=SIN_SCALE).then_inc(s_trig, 1)
                act.wait_ge(s_stm, b + 1)
                if b:
                    act.wait_ge(s_yps, b)
                for r in range(2):
                    A(BT[:, r].rearrange("p g m -> p (g m)"), ps[:, 4 + r, :], ACT.Copy)
                A(TP.rearrange("p g m -> p (g m)"), ps[:, 6, :], ACT.Copy).then_inc(s_ste, 1)
                for u in range(FIRST["za"] + 2 * b, FIRST["za"] + 2 * b + 2):
                    evac(u)
                act.wait_ge(s_ysm, b + 1)
                for j in range(4):
                    for s in range(SUB):
                        dst = yaT[32 * j:32 * j + 32, b, :].rearrange("p (c s) -> p s c", s=SUB)[:, s, :]
                        last = A(dst, U[32 * s:32 * s + 32, BATCH_PAIRS * b + j, :], ACT.Gelu_apprx_tanh)
                last.then_inc(s_ya, 1)
            act.wait_ge(s_yps, 4)
            evacs("glu")
            evacs("ga0")
            evacs("ga1")
            evacs("ao")
            evacs("q")
            evacs("zb")
            act.wait_ge(s_comb, 24)
            attention(s_att[0], items1, groups1, at1)
            act.wait_ge(s_att[0]["yT_used"], 8)
            evacs("gb0")
            evacs("gb1")
            evacs("bo")
            act.wait_ge(s_att[0]["yT"], 8)
            evacs("gate0")
            evacs("gate1")
            act.wait_ge(s_comb, 40)
            evacs("out0")
            evacs("out1")
            act.wait_ge(s_comb, 56)
            squares(XR, s_ssq, lambda t: hT[:, t, :])
            act.wait_ge(s_mean, 2)
            A(rs, rs, ACT.Sqrt).then_inc(s_root, 1)

            for n in range(16):
                act.wait_ge(s_xt2, n + 1)
                A(hT[:, n // 2, (n % 2) * 512:(n % 2) * 512 + 512], ps[:, 4 + n % 4, :], ACT.Copy).then_inc(s_ht2, 1)
            evacs("dt")
            act.wait_ge(s_dtv, 1)
            link(A(dtv, dtv, ACT.Exp, scale=-1.0))
            A(aexp, par("alog"), ACT.Exp)
            A(dtv, dtv, ACT.Ln, bias=1.0).then_inc(s_dta, 1)

            def activate(ct):
                act.wait_ge(s_conv, ct + 1)
                if 2 <= ct < 8:
                    act.wait_ge(s_ct, ct - 1)
                dst = cxs[ct % 2] if ct < 8 else (BTf[:, ct - 8, :] if ct < 10 else CTf[:, ct - 10, :])
                A(dst, acc[ct % 2], ACT.Silu, bias=par("convb")[:, ct:ct + 1]).then_inc(s_silu, 1)

            for ct in range(CONV_TILES):
                for half in range(2):
                    evac(FIRST["xbc0"] + 2 * ct + half)
                if ct >= 1:
                    activate(ct - 1)
            activate(CONV_TILES - 1)
            act.wait_ge(s_x2st, 16 * NT)
            evacs("zs0")
            evacs("zs1")
            act.wait_ge(s_cum, 1)
            A(cst, ps[:, 6, 0:128], ACT.Copy)
            A(ctot, ps[:, 6, 128:256], ACT.Exp)
            A(ecs, ps[:, 6, 0:128], ACT.Exp).then_inc(s_cume, 1)
            act.wait_ge(s_dtv, 4)
            A(dte, dte, ACT.Exp).then_inc(s_cume, 1)
            for m in range(16):
                act.wait_ge(s_dif, m + 1)
                if m:
                    act.wait_ge(s_yd, m)
                A(dec[:], dif[:], ACT.Exp).then_inc(s_dec, 1)
            act.wait_ge(s_yo, 16)
            squares(Z, s_nrm["ssm"][0], lambda t: dif_flat)
            act.wait_ge(s_nrm["ssm"][1], 1)
            A(rs, rs, ACT.Sqrt).then_inc(s_nrm["ssm"][2], 1)
            act.wait_ge(s_nrm["ssm"][5], 16)
            evacs("pair0")

            def next_pair(n):
                j, step = n // 16 + 1, n % 16
                if j < 8 and step in PAIR_UNIT_STEPS:
                    evac(FIRST[f"pair{j}"] + PAIR_UNIT_STEPS.index(step))

            attention(s_att[1], items2, groups2, at2, next_pair)
            act.wait_ge(s_att[1]["read"], 16)
            squares(YA, s_nrm["att"][0], lambda t: mixA[:, t, :])
            act.wait_ge(s_nrm["att"][1], 1)
            A(rs, rs, ACT.Sqrt).then_inc(s_nrm["att"][2], 1)
            act.wait_ge(s_free, len(UNITS))
            for t in range(NT):
                last = A(hT[:, t, :], res[:, t, :], ACT.Copy, accum_out=ss[:, t:t + 1])
            last.then_inc(s_ln[0], 1)
            act.wait_ge(s_ln[1], 1)
            for t in range(NT):
                last = A(mixA[:, t, :], res[:, t, :], ACT.Square, bias=nmu[:, t:t + 1], accum_out=ss[:, t:t + 1])
            last.then_inc(s_ln[2], 1)
            act.wait_ge(s_ln[3], 1)
            A(rs, rs, ACT.Sqrt).then_inc(s_ln[4], 1)

        @block.vector
        def _(dve):
            chain = [0]
            V = nc.vector

            def link(ins):
                chain[0] += 1
                ins.then_inc(s_v, 1)
                dve.wait_ge(s_v, chain[0])

            def mult(o, a, b):
                return V.tensor_tensor(o, a, b, ALU.mult)

            def norm_scale(squares_in, mean_out, root_in, eps):
                dve.wait_ge(squares_in[0], squares_in[1])
                V.tensor_scalar(rs, ss, 1.0 / D, eps, ALU.mult, ALU.add).then_inc(mean_out, 1)
                dve.wait_ge(root_in[0], root_in[1])
                link(V.reciprocal(rs, rs))

            def attention(sems, items, groups, tiles, bias_of, close):
                def copies(n):
                    for g, b0, nb in groups[n]:
                        dve.wait_ge(sems["transposed"], g + 1)
                        if g >= 2:
                            dve.wait_ge(sems["weighted"], g - 1)
                        V.tensor_copy(tiles["pt"][g % 2][:, 0:nb * P], ps[:, 4 + g % 2, 0:nb * P])\
                            .then_inc(sems["copied"], 1)

                for n in range(len(items) + 2):
                    if n < len(items):
                        dve.wait_ge(sems["scores"], n + 1)
                        if n >= 2:
                            dve.wait_ge(sems["transposed"], groups[n - 2][-1][0] + 1)
                        keys = P * (items[n][2] + 1)
                        V.tensor_tensor_reduce(tiles["sbuf"][n % 2][:, 0:keys],
                                               ps[:, 2:4, :].rearrange("p a b -> p (a b)")[:, 0:keys], bias_of(items[n]),
                                               1.0, BIG, ALU.add, ALU.min,
                                               mneg4[:, n % 4:n % 4 + 1]).then_inc(sems["biased"], 1)
                    if 1 <= n <= len(items):
                        copies(n - 1)
                    if n >= 2 and items[n - 2][1] == 7:
                        outer = items[n - 2][0]
                        dve.wait_ge(sems["weighted"], groups[n - 2][-1][0] + 1)
                        r8 = rden[:, (outer % 2) * 8:(outer % 2) * 8 + 8]
                        link(V.reciprocal(r8, den[:, (outer % 2) * 8:(outer % 2) * 8 + 8]))
                        close(outer, ps[:, 6 + outer % 2, :].rearrange("p (a d) -> p a d", a=8),
                              r8.unsqueeze(2).to_broadcast([P, 8, DH]))

            dve.wait_ge(s_par, 32)
            V.memset(half_pi, HALF_PI)
            norm_scale((s_ssq, 1), s_mean, (s_root, 1), RMS_EPS)
            for t in range(NT):
                V.tensor_scalar(XR0[:, t, :], XR0[:, t, :], rs[:, t:t + 1], None, ALU.mult).then_inc(s_xn, 1)
            dve.wait_ge(s_free, 4)
            V.tensor_tensor(shf, modv[:, 0:8], par("bshift"), ALU.add)
            link(V.tensor_tensor(sc1, modv[:, 8:16], par("bscale"), ALU.add))
            link(V.scalar_tensor_tensor(sc1, sc1, 1.0, par("normg"), ALU.add, ALU.mult))
            for n in range(16):
                k = n // 2
                dve.wait_ge(s_xt, n + 1)
                V.tensor_scalar(hT[:, k, (n % 2) * 512:(n % 2) * 512 + 512], ps[:, 4 + n % 4, :], sc1[:, k:k + 1],
                                shf[:, k:k + 1], ALU.mult, ALU.add).then_inc(s_ht, 1)

            dve.wait_ge(s_prm, 1)
            mult(ard, par("ar"), dts)
            link(mult(aid, par("ai"), dts))
            link(V.tensor_scalar(kk, aid, 1.0 / TWO_PI, None, ALU.mult))
            link(V.tensor_scalar(kk, kk, ROUND, None, ALU.add))
            link(V.tensor_scalar(kk, kk, ROUND, None, ALU.subtract))
            link(V.scalar_tensor_tensor(th, kk, -PI2_A, aid, ALU.mult, ALU.add))
            link(V.scalar_tensor_tensor(th, kk, -PI2_B, th, ALU.mult, ALU.add))
            link(V.scalar_tensor_tensor(th, kk, -PI2_C, th, ALU.mult, ALU.add))
            link(V.tensor_scalar(th, th, 3.1415925, -3.1415925, ALU.min, ALU.max))
            link(V.tensor_scalar(frac, th, SUB / TWO_PI, None, ALU.mult))
            link(V.tensor_scalar(kk, frac, ROUND, None, ALU.add))
            link(V.tensor_scalar(kk, kk, ROUND, None, ALU.subtract))
            V.tensor_tensor(frac, frac, kk, ALU.subtract)
            link(V.tensor_scalar(r2, th, -1.0, None, ALU.mult))
            V.tensor_tensor(r2, r2, th, ALU.max).then_inc(s_prv, 1)
            dve.wait_ge(s_prm, 3)
            V.memset(pw[:, 0, 0, :], 1.0)
            V.memset(pw[:, 1, 0, :], 0.0)
            mult(pw[:, 0, 1, :], r1, r2)
            link(mult(pw[:, 1, 1, :], r1, th))
            for k, (a, b) in ((2, (1, 1)), (3, (2, 1)), (4, (2, 2))):
                mult(r1, pw[:, 0, a, :], pw[:, 0, b, :])
                mult(r2, pw[:, 1, a, :], pw[:, 1, b, :])
                mult(kk, pw[:, 0, a, :], pw[:, 1, b, :])
                link(mult(th, pw[:, 1, a, :], pw[:, 0, b, :]))
                V.tensor_tensor(pw[:, 0, k, :], r1, r2, ALU.subtract)
                link(V.tensor_tensor(pw[:, 1, k, :], kk, th, ALU.add))
            mult(r1, par("ar"), par("ar"))
            link(mult(r2, par("ai"), par("ai")))
            link(V.tensor_tensor(r1, r1, r2, ALU.add))
            link(V.reciprocal(dts, r1))
            link(V.tensor_scalar(kk, pw[:, 0, 1, :], 1.0, None, ALU.subtract))
            mult(r1, kk, par("ar"))
            mult(r2, pw[:, 1, 1, :], par("ai"))
            mult(th, pw[:, 1, 1, :], par("ar"))
            link(mult(aid, kk, par("ai")))
            V.tensor_tensor(r1, r1, r2, ALU.add)
            link(V.tensor_tensor(th, th, aid, ALU.subtract))
            mult(coef[:, 0, :], r1, dts)
            mult(coef[:, 1, :], th, dts).then_inc(s_prv, 1)
            dve.wait_ge(s_prv, 2)
            bb = area(30728, 512, "p (r g q) -> p r g q", r=2, g=PAIRS)
            t256 = area(28672, 512, "p (r g q) -> p r g q", r=2, g=PAIRS)
            br = par("br").rearrange("p (g q) -> p g q", g=PAIRS)
            bi = par("bi").rearrange("p (g q) -> p g q", g=PAIRS)
            co = [coef[:, r, :].unsqueeze(2).to_broadcast([P, PAIRS, PG]) for r in range(2)]
            mult(t256[:, 0], br, co[0])
            link(mult(t256[:, 1], bi, co[1]))
            link(V.tensor_tensor(bb[:, 0], t256[:, 0], t256[:, 1], ALU.subtract))
            mult(t256[:, 0], bi, co[0])
            link(mult(t256[:, 1], br, co[1]))
            link(V.tensor_tensor(bb[:, 1], t256[:, 0], t256[:, 1], ALU.add))
            link(V.memset(BH[:], 0.0))
            for r in range(2):
                last = V.memset(Gs[r][:], 0.0)
            last.then_inc(s_prv, 1)
            dve.wait_ge(s_prv, 3)

            n = 0
            for i in range(2, NT):
                for h in range(HEADS1):
                    keys = P * (i + 1)
                    dve.wait_ge(s_ixr, n + 1)
                    w = vw[:, i, 64 + h:65 + h]
                    if h == 0:
                        V.tensor_scalar(sc_at(i), relu_sl[n % 2][:, 0:keys], w, None, ALU.mult).then_inc(s_ixa, 1)
                    else:
                        dve.wait_ge(s_ixa, n)
                        V.scalar_tensor_tensor(sc_at(i), relu_sl[n % 2][:, 0:keys], w, sc_at(i), ALU.mult,
                                               ALU.add).then_inc(s_ixa, 1)
                    n += 1
                dve.wait_ge(s_ixa, n)
                diag = sc_at(i)[:, P * i:P * (i + 1)]
                link(V.tensor_tensor(diag, diag, con("ahead_fill"), ALU.add))
            link(V.memset(SC[:, 0:3 * P], 0.0))
            V.tensor_copy(sc_at(0), con("ahead_big"))
            link(V.tensor_copy(sc_at(1)[:, P:2 * P], con("ahead_big")))

            for b in range(4):
                gs = slice(BATCH_PAIRS * b, BATCH_PAIRS * (b + 1))
                t1, t2 = (area(31240 + 64 * q, 64, "p (g q) -> p g q", g=BATCH_PAIRS) for q in range(2))
                if b:
                    dve.wait_ge(s_yps, b)
                for s in range(SUB):
                    k = 3 - s
                    er = pw[:, 0, k, gs].unsqueeze(2).to_broadcast([P, BATCH_PAIRS, PG])
                    ei = pw[:, 1, k, gs].unsqueeze(2).to_broadcast([P, BATCH_PAIRS, PG])
                    for r in range(2):
                        mult(t1, bb[:, r, gs], er)
                        link(mult(t2, bb[:, 1 - r, gs], ei))
                        for half in range(2):
                            rows_, cols = slice(64 * half, 64 * half + 64), slice(PG * half, PG * half + PG)
                            last = V.tensor_tensor(BH[rows_, r, :, s, cols], t1[rows_], t2[rows_],
                                                   ALU.add if r else ALU.subtract)
                        if (s, r) == (3, 1):
                            last.then_inc(s_bh, 1)
                        else:
                            link(last)
                dve.wait_ge(s_zin, b + 1)
                dve.wait_ge(s_trig, b + 1)
                zr = ps[:, 4:6, :].rearrange("p a b -> p (a b)")
                zi = ps[:, 6:8, :].rearrange("p a b -> p (a b)")

                def by_pair(v):
                    return v.rearrange("p (g c) -> p g c", g=BATCH_PAIRS)

                gr, gi = Gs[0][:, :, 1:257], Gs[1][:, :, 1:257]
                mult(rot_a, zr, cosT)
                link(mult(rot_b, zi, sinT))
                link(V.tensor_tensor(gr, by_pair(rot_a), by_pair(rot_b), ALU.add))
                mult(rot_a, zi, cosT)
                link(mult(rot_b, zr, sinT))
                link(V.tensor_tensor(gi, by_pair(rot_a), by_pair(rot_b), ALU.subtract))
                for g in range(BATCH_PAIRS):
                    d0 = rho[:, BATCH_PAIRS * b + g:BATCH_PAIRS * b + g + 1].to_broadcast([P, NCH])
                    for G in (gr, gi):
                        last = V.tensor_tensor_scan(G[:, g, :], d0, G[:, g, :], 0.0, ALU.mult, ALU.add)
                link(last)
                mult(by_pair(rot_a), gr, by_pair(cosT))
                link(mult(by_pair(rot_b), gi, by_pair(sinT)))
                mult(gi, gi, by_pair(cosT))
                link(mult(gr, gr, by_pair(sinT)))
                link(V.tensor_tensor(gi, gi, gr, ALU.add))
                V.tensor_tensor(gr, by_pair(rot_a), by_pair(rot_b), ALU.subtract).then_inc(s_hout, 1)
                dve.wait_ge(s_yps, b + 1)
                for g in range(BATCH_PAIRS):
                    q = BATCH_PAIRS * b + g
                    last = V.scalar_tensor_tensor(U[:, q, :], U[:, q, :], par("dskip")[:, q:q + 1],
                                                  ps[:, 4 + g // 2, (g % 2) * NCH:(g % 2 + 1) * NCH], ALU.mult, ALU.add)
                last.then_inc(s_ysm, 1)

            for i in range(2, NT):
                for _ in range(TOPK // 8):
                    link(V.max(mx, sc_at(i)))
                    link(V.match_replace(sc_at(i), mx, sc_at(i), TAKEN))
                V.tensor_scalar(sc_at(i), sc_at(i), TAKEN_LIMIT, BIG, ALU.is_gt, ALU.mult).then_inc(s_mask, 1)
            dve.wait_ge(s_mask, 6)
            dve.wait_ge(s_comb, 24)

            def close1(i, o, r):
                if i >= 2:
                    dve.wait_ge(s_att[0]["yT"], i - 1)
                y = ytile[:, (i % 2) * 512:(i % 2) * 512 + 512]
                mult(y.rearrange("p (a d) -> p a d", a=8), o, r).then_inc(s_att[0]["read"], 1)
                if i >= 1:
                    gate_rows(i - 1)

            def gate_rows(i):
                dve.wait_ge(s_att[0]["yT"], i + 1)
                mult(ybT[:, :, i * P:(i + 1) * P], ps[:, i % 2, :].rearrange("p (f t) -> p f t", f=4),
                     zbT[:, :, i * P:(i + 1) * P]).then_inc(s_att[0]["yT_used"], 1)

            attention(s_att[0], items1, groups1, at1, lambda it: sc_at(it[2]), close1)
            gate_rows(7)
            dve.wait_ge(s_free, unit_end("gate1"))
            dve.wait_ge(s_row, 32)
            V.tensor_tensor(gate, gate, bgate, ALU.add).then_inc(s_gate, 1)
            norm_scale((s_ssq, 2), s_mean, (s_root, 2), RMS_EPS)
            for t in range(NT):
                V.scalar_tensor_tensor(XR[:, t, :], XR[:, t, :], rs[:, t:t + 1], frow, ALU.mult, ALU.mult)\
                    .then_inc(s_x2, 1)

            def by_chunk(v):
                return v.rearrange("p (c h) -> p c h", h=16)

            dve.wait_ge(s_ht2, 16)
            for s in range(2):
                link(V.memset(raw[s][:, 0:3], 0.0))
            dve.wait_ge(s_free, unit_end("dt"))
            link(V.tensor_tensor(by_chunk(dtr), by_chunk(dtr), par("dtb").unsqueeze(1).to_broadcast([P, NT, 16]),
                                 ALU.add))
            link(V.tensor_scalar(dtv, dtr, -1.0, None, ALU.mult))
            V.tensor_tensor(dtv, dtv, dtr, ALU.max).then_inc(s_dtv, 1)
            dve.wait_ge(s_dta, 1)
            link(V.scalar_tensor_tensor(dtv, dtr, 0.0, dtv, ALU.max, ALU.add))
            link(mult(by_chunk(adt), by_chunk(dtv), aexp.unsqueeze(1).to_broadcast([P, NT, 16])))
            V.tensor_scalar(adt, adt, -1.0, None, ALU.mult).then_inc(s_dtv, 2)

            def place(ct):
                dve.wait_ge(s_ct, ct + 1)
                src = ps[:, 4 + 2 * (ct % 2):6 + 2 * (ct % 2), :].rearrange("p a (t c) -> p (a t) c", t=4)
                dst = xs[:, :, ct * P:(ct + 1) * P] if ct < 8 else Btok[:, :, ct - 8, :]
                V.tensor_copy(dst, src).then_inc(s_xs, 1)

            for ct in range(CONV_TILES):
                dve.wait_ge(s_free, FIRST["xbc0"] + 2 * ct + 2)
                if ct >= 2:
                    dve.wait_ge(s_silu, ct - 1)
                a = acc[ct % 2]
                link(V.tensor_scalar(a, raw[ct % 2][:, 0:1024], par("convw")[:, 4 * ct:4 * ct + 1], None, ALU.mult))
                for w in range(1, 4):
                    ins = V.scalar_tensor_tensor(a, raw[ct % 2][:, w:w + 1024],
                                                 par("convw")[:, 4 * ct + w:4 * ct + w + 1], a, ALU.mult, ALU.add)
                    if w < 3:
                        link(ins)
                    else:
                        ins.then_inc(s_conv, 1)
                if ct >= 2:
                    place(ct - 2)

            dve.wait_ge(s_conv, CONV_TILES)
            dve.wait_ge(s_silu, CONV_TILES)
            V.memset(hst, 0.0).then_inc(s_st, 1)
            dve.wait_ge(s_cume, 1)
            V.tensor_tensor(dte, ps[:, 6, 128:256], cst, ALU.subtract).then_inc(s_dtv, 1)
            dve.wait_ge(s_cume, 2)
            dve.wait_ge(s_silu, 12)
            for m in range(16):
                c, g = m // 2, m % 2
                hs = slice(c * 16 + g * 8, c * 16 + g * 8 + 8)

                def per_head(v, w=DH):
                    return v[:, hs].unsqueeze(2).to_broadcast([P, 8, w])

                def heads(v):
                    return v.rearrange("p (h d) -> p h d", h=8)

                dve.wait_ge(s_csb, m + 1)
                if m:
                    dve.wait_ge(s_dec, m)
                    dve.wait_ge(s_mt, m)
                link(V.tensor_tensor(dif, ps[:, 0:2, :].rearrange("p a (h l) -> p (a h) l", h=4), per_head(cst, CHUNK),
                                     ALU.subtract))
                V.tensor_scalar(dif[:], dif[:], 0.0, None, ALU.min)
                mult(cbm, ps[:, 2, 0:P], tri).then_inc(s_dif, 1)
                x_ = xs[:, c, g * 512:g * 512 + 512]
                link(mult(heads(xg[:, 0:512]), heads(x_), per_head(dtv)))
                mult(heads(xgd[:, 0:512]), heads(xg[:, 0:512]), per_head(dte)).then_inc(s_xg, 1)
                dve.wait_ge(s_yd, m + 1)
                y = yt[:, 0:512]
                link(mult(heads(y), heads(ps[:, 4, :]), per_head(ecs)))
                mult(heads(yt2), heads(x_), par("dskip2")[:, g * 8:g * 8 + 8].unsqueeze(2).to_broadcast([P, 8, DH]))
                link(V.tensor_tensor(y, y, ps[:, 3, :], ALU.add))
                link(V.tensor_tensor(y, y, yt2, ALU.add))
                z_ = Z[:, c, g * 512:g * 512 + 512]
                mult(z_, z_, y)
                H = hst[:, g * 512:g * 512 + 512]
                link(mult(heads(H), heads(H), per_head(ctot)))
                V.tensor_tensor(H, H, ps[:, 5, :], ALU.add).then_inc(s_yo, 1)
            dve.wait_ge(s_yo, 16)

            def norm_rows(src, dst, gains, sems):
                norm_scale((sems[0], 1), sems[1], (sems[2], 1), NORM_EPS)
                for t in range(NT):
                    V.tensor_scalar(src[:, t, :], src[:, t, :], rs[:, t:t + 1], None, ALU.mult).then_inc(sems[3], 1)
                for n in range(16):
                    dve.wait_ge(sems[4], n + 1)
                    V.tensor_scalar(dst[:, n // 2, (n % 2) * 512:(n % 2) * 512 + 512], ps[:, 4 + n % 4, :],
                                    gains[:, n // 2:n // 2 + 1], None, ALU.mult).then_inc(sems[5], 1)

            norm_rows(Z, mixS, par("ssmg"), s_nrm["ssm"])
            dve.wait_ge(s_alibi, 32)

            def bias2(it):
                h, i = it[3], it[2]
                t = TB[h % 2]
                if it[1] == 0:
                    link(V.scalar_tensor_tensor(t, dist, SLOPES[h], nlog, ALU.mult, ALU.add))
                return t[:, 896 - P * i:1024]

            def close2(h, o, r):
                j = h // 2
                dve.wait_ge(s_zs, j + 1)
                y = YA[:, :, h * DH:(h + 1) * DH]
                link(mult(y, o, r))
                mult(y, y, pz[j % 2][:, :, DH * (h % 2):DH * (h % 2) + DH])\
                    .then_inc(s_att[1]["read"], 1)

            attention(s_att[1], items2, groups2, at2, bias2, close2)
            norm_rows(YA, mixA, par("attg"), s_nrm["att"])
            dve.wait_ge(s_xr, 32)
            for u in range(FIRST["wo0"], len(UNITS)):
                name, i = UNITS[u]
                j = int(name[2])
                dve.wait_ge(s_unit, u + 1)
                v = res[:, 2 * i:2 * i + 2, j * 256:(j + 1) * 256]
                V.scalar_tensor_tensor(v, v, ALPHA, ps[:, unit_bank(u), :].rearrange("p (t c) -> p t c", t=2),
                                       ALU.mult, ALU.add).then_inc(s_free, 1)
            dve.wait_ge(s_ln[0], 1)
            V.tensor_scalar(nmu, ss, -1.0 / D, None, ALU.mult).then_inc(s_ln[1], 1)
            dve.wait_ge(s_ln[2], 1)
            V.tensor_scalar(rs, ss, 1.0 / D, NORM_EPS, ALU.mult, ALU.add).then_inc(s_ln[3], 1)
            dve.wait_ge(s_ln[4], 1)
            link(V.reciprocal(rs, rs))
            dve.wait_ge(s_row, 64)
            for t in range(NT):
                link(V.tensor_scalar(res[:, t, :], res[:, t, :], nmu[:, t:t + 1], rs[:, t:t + 1], ALU.add, ALU.mult))
                link(mult(res[:, t, :], res[:, t, :], lng))
                V.tensor_tensor(res[:, t, :], res[:, t, :], lnb, ALU.add).then_inc(s_ln[5], 1)


def arrange(inputs):
    a = {k: np.asarray(v) for k, v in inputs.items()}
    w_in, w_in2 = a["w_in"][0], a["w_in_2"][0]

    def tiles(w, cols=None):
        k = w.shape[0] // P
        o = np.zeros((P, k, LOADW // k), np.float32)
        o[:, :, :w.shape[1]] = w.reshape(k, P, w.shape[1]).transpose(1, 0, 2)
        return o.reshape(P, LOADW)

    at = {}
    pos = 0
    for name, n in (("xa", 512), ("za", 512), ("q", 512), ("k", 64), ("v", 64), ("zb", 512), ("qi", 512), ("ki", 64),
                    ("wi", 8), ("ga", 1024), ("gb", 1024)):
        at[name] = w_in[:, pos:pos + n]
        pos += n
    q2, k2, v2, z2, zs2, xbc2, dt2 = np.split(w_in2, np.cumsum([1024, 1024, 1024, 1024, 1024, 1536]), axis=1)
    made = {
        "small": np.concatenate([at["k"], at["k"], at["ki"], at["ki"], at["v"], at["wi"]], axis=1),
        "qi": at["qi"], "xa": at["xa"], "za": at["za"], "q": at["q"], "zb": at["zb"],
        "glu": a["w_glu"][0], "ao": a["w_a_o"][0], "bo": a["w_b_o"][0], "dt": dt2}
    for n in range(6):
        made[f"mod{n}" if n < 4 else f"gate{n - 4}"] = a["w_mod"][0][:, 512 * n:512 * n + 512]
    for n in range(2):
        cols = slice(512 * n, 512 * n + 512)
        made[f"ga{n}"], made[f"gb{n}"] = at["ga"][:, cols], at["gb"][:, cols]
        made[f"out{n}"], made[f"zs{n}"] = a["w_out"][0][:, cols], zs2[:, cols]
    for n in range(3):
        made[f"xbc{n}"] = xbc2[:, 512 * n:512 * n + 512]
    for j in range(8):
        cols = slice(128 * j, 128 * j + 128)
        made[f"pair{j}"] = np.concatenate([q2[:, cols], k2[:, cols], v2[:, cols], z2[:, cols]], axis=1)
    for j in range(4):
        made[f"wo{j}"] = a["w_out_2"][0][:, 256 * j:256 * j + 256]
    loads = np.stack([tiles(made[n]) for n in LOADS])

    params = np.zeros((P, NPARAM), np.float32)

    def put(name, v):
        params[:, PARAMS[name]] = v

    def by_state(v):
        return v.reshape(16, 2, 64).transpose(1, 2, 0).reshape(P, 16)

    def by_feature(v):
        return v.reshape(-1, P).T

    put("ar", by_state(a["a_re"][0]))
    put("ai", by_state(a["a_im"][0]))
    put("ldt", by_state(np.repeat(a["log_dt"][0][:, None], 64, axis=1)))
    for n, s in (("br", "b_re"), ("bi", "b_im")):
        put(n, a[s][0].reshape(16, 2, 64, PG).transpose(1, 2, 0, 3).reshape(P, 256))
    for n, s in (("cr", "c_re"), ("ci", "c_im")):
        put(n, a[s][0].reshape(16, 2, PG, 64).transpose(1, 3, 0, 2).reshape(P, 256))
    put("dskip", np.tile(a["d_skip"][0].reshape(16, 32).T, (4, 1)))
    put("c", by_feature(a["c"][0]))
    put("normg", by_feature(a["norm_g"][0]))
    put("bshift", by_feature(a["b_mod"][0][:1024]))
    put("bscale", by_feature(a["b_mod"][0][1024:2048]))
    put("bglu", by_feature(a["b_glu"][0]))
    put("convw", a["conv_w_2"][0].T.reshape(12, P, 4).transpose(1, 0, 2).reshape(P, 48))
    put("convb", by_feature(a["conv_b_2"][0]))
    for n, s in (("dtb", "dt_bias_2"), ("alog", "a_log_2"), ("dskip2", "d_skip_2")):
        put(n, np.broadcast_to(a[s][0], (P, 16)))
    put("attg", by_feature(a["att_norm_g_2"][0]))
    put("ssmg", by_feature(a["ssm_norm_g_2"][0]))
    rows = np.ascontiguousarray(np.broadcast_to(np.stack(
        [a["b_mod"][0][2048:], a["final_g"], a["ln_g_2"][0], a["ln_b_2"][0]])[:, None, :], (4, P, D)))

    r = np.arange(P)
    consts = np.zeros((P, NCONST), np.float32)
    ahead = (r[None, :] > r[:, None]).astype(np.float32)
    for name, v in (("ident", np.eye(P)), ("tri", r[:, None] <= r[None, :]), ("ones", 1.0),
                    ("step", np.arange(NCH)[None, :]), ("ahead_fill", ahead * CAUSAL_FILL), ("ahead_big", ahead * BIG)):
        consts[:, CONSTS[name]] = v
    d = r[:, None] + 896 - np.arange(SEQ)[None, :]
    times = sum(((d >= 0) & (d % s == 0) & (d <= 128 * s)).astype(np.float64) for s in (1, 4, 16))
    alibi = np.stack([d, np.where(times > 0, -np.log(np.maximum(times, 1)), BIG)]).astype(np.float32)
    return {"x": a["x"][0], "loads": loads, "params": params, "consts": consts, "rows": rows, "alibi": alibi}


def kernel(**inputs):
    import numpy as _np
    import concourse.bacc as _bacc
    from concourse import mybir as _mybir
    from concourse.bass_utils import run_bass_kernel_spmd as _run

    nc = _bacc.Bacc("TRN2", target_bir_lowering=False, num_devices=1)
    arrays, args = {}, []
    for name, v in arrange(inputs).items():
        v = _np.ascontiguousarray(v)
        arrays[f"in_{name}"] = v
        args.append(nc.dram_tensor(f"in_{name}", v.shape, _mybir.dt.float32, kind="ExternalInput").ap())
    out = nc.dram_tensor("out_0", (SEQ, D), _mybir.dt.float32, kind="ExternalOutput").ap()
    x2 = nc.dram_tensor("x2_scratch", (NT, P, D), _mybir.dt.float32, kind="Internal").ap()
    layer_kernel(nc, *args, out, x2)
    r = _run(nc, [arrays], core_ids=[0])
    return r.results[0]["out_0"].reshape(1, SEQ, D)
```
